# Optimizing a Trainium2 kernel written in Bass

```python
import jax, jax.numpy as jnp
from jax import lax
import numpy as np
import math

D_MODEL = 2048
BATCH = 1
SEQ = 256
DEPTH = 1

CTX_LEN = 256
GRID_W = 64
MIX_W = D_MODEL
HEAD_SIZE = 128
ATTN_W = MIX_W // 2
N_HEADS = ATTN_W // HEAD_SIZE
QK_NOPE = 128
QK_ROPE = 64
V_DIM = HEAD_SIZE
Q_RANK = D_MODEL // 4
KV_RANK = D_MODEL // 8
CONV_W = MIX_W - ATTN_W
CONV_GROUPS = CONV_W // HEAD_SIZE
N_GROUPS = MIX_W // HEAD_SIZE
FFN_DIM = ((8 * D_MODEL // 3 + 127) // 128) * 128
IN_COLS = Q_RANK + KV_RANK + QK_ROPE + 3 * CONV_W
ROPE_BASE = 10000.0
Q_BLOCK = 128
EPS = 1e-6


def rms_norm(x, g):
    xf = x.astype(jnp.float32)
    y = xf * lax.rsqrt(jnp.mean(xf * xf, axis=-1, keepdims=True) + EPS)
    return (y * g.astype(jnp.float32)).astype(x.dtype)

def modulate(h, shift, scale):
    return h * (1 + scale) + shift

def axial_rope_tables(n_tok, dtype):
    rows = n_tok // GRID_W
    row = jnp.repeat(jnp.arange(rows), GRID_W).astype(jnp.float32)
    col = jnp.tile(jnp.arange(GRID_W), rows).astype(jnp.float32)
    axis_dim = QK_ROPE // 2
    inv = ROPE_BASE ** (-jnp.arange(0, axis_dim, 2, dtype=jnp.float32) / axis_dim)
    ang = jnp.concatenate([row[:, None] * inv, col[:, None] * inv], axis=-1)
    return jnp.cos(ang).astype(dtype), jnp.sin(ang).astype(dtype)

def apply_rope(x, cos, sin):
    xp = x.reshape(*x.shape[:-1], QK_ROPE // 2, 2)
    x1, x2 = xp[..., 0], xp[..., 1]
    return jnp.stack([x1 * cos - x2 * sin, x1 * sin + x2 * cos], axis=-1).reshape(x.shape)

def dwconv3(x, w, b):
    xp = jnp.pad(x, ((0, 0), (1, 1), (0, 0)))
    return xp[:, :-2] * w[0] + xp[:, 1:-1] * w[1] + xp[:, 2:] * w[2] + b

def split_projection(p):
    cuts = [Q_RANK, Q_RANK + KV_RANK, Q_RANK + KV_RANK + QK_ROPE,
            Q_RANK + KV_RANK + QK_ROPE + CONV_W, Q_RANK + KV_RANK + QK_ROPE + 2 * CONV_W]
    return jnp.split(p, cuts, axis=-1)

def mla_query(q_a, g_q_a, w_q_b, rope):
    b, l, _ = q_a.shape
    q = (rms_norm(q_a, g_q_a) @ w_q_b).reshape(b, l, N_HEADS, QK_NOPE + QK_ROPE).transpose(0, 2, 1, 3)
    q_nope, q_rope = q[..., :QK_NOPE], q[..., QK_NOPE:]
    if rope is not None:
        q_rope = apply_rope(q_rope, *rope)
    return jnp.concatenate([q_nope, q_rope], axis=-1)

def mla_key_value(kv_a, k_rope, g_kv_a, w_kv_b, rope):
    b, l, _ = kv_a.shape
    kv = (rms_norm(kv_a, g_kv_a) @ w_kv_b).reshape(b, l, N_HEADS, QK_NOPE + V_DIM).transpose(0, 2, 1, 3)
    k_nope, v = kv[..., :QK_NOPE], kv[..., QK_NOPE:]
    if rope is not None:
        k_rope = apply_rope(k_rope, *rope)
    k_rope = jnp.broadcast_to(k_rope[:, None], (b, N_HEADS, l, QK_ROPE))
    return jnp.concatenate([k_nope, k_rope], axis=-1), v

def block_attention(q, k, v):
    b, h, l, dqk = q.shape
    nb = l // Q_BLOCK
    scale = (QK_NOPE + QK_ROPE) ** -0.5
    qb = q.reshape(b, h, nb, Q_BLOCK, dqk).transpose(2, 0, 1, 3, 4)

    def one_block(qi):
        s = jnp.einsum("bhqd,bhkd->bhqk", qi, k).astype(jnp.float32) * scale
        p = jax.nn.softmax(s, axis=-1).astype(v.dtype)
        return jnp.einsum("bhqk,bhkd->bhqd", p, v)

    o = lax.map(one_block, qb)
    return o.transpose(1, 0, 3, 2, 4).reshape(b, l, h * V_DIM)

def short_conv(gate_b, gate_c, hc, w, bias):
    return gate_b * dwconv3(gate_c * hc, w, bias)

def merge_heads(att, conv, g_mix, w_out):
    b, l, _ = att.shape
    mix = jnp.concatenate([att, conv], axis=-1).reshape(b, l, N_GROUPS, HEAD_SIZE)
    mix = rms_norm(mix, g_mix.reshape(N_GROUPS, HEAD_SIZE)).reshape(b, l, MIX_W)
    return mix @ w_out

def conv_ffn(h, w_up, cw, cb, w_down):
    u = dwconv3(h @ w_up, cw, cb)
    a, g = jnp.split(u, 2, axis=-1)
    return (a * jax.nn.silu(g)) @ w_down

def first_inputs(seed: int = 0) -> dict:
    key = jax.random.key(seed)
    ks = jax.random.split(key, 24)
    f32 = jnp.float32
    nrm = lambda k, shape, s: jax.random.normal(k, shape, f32) * s
    gain = lambda k, shape: 1.0 + 0.02 * jax.random.normal(k, shape, f32)
    return {
        "x": nrm(ks[0], (BATCH, SEQ, D_MODEL), 1.0),
        "c": nrm(ks[1], (BATCH, D_MODEL), 1.0),
        "ctx": nrm(ks[2], (BATCH, CTX_LEN, D_MODEL), 1.0),
        "c_ctx": nrm(ks[3], (D_MODEL,), 1.0),
        "w_ada": nrm(ks[4], (DEPTH, D_MODEL, 6 * D_MODEL), D_MODEL ** -0.5),
        "b_ada": nrm(ks[5], (DEPTH, 6 * D_MODEL), 0.01),
        "g_mix_norm": gain(ks[6], (DEPTH, D_MODEL)),
        "w_in": nrm(ks[7], (DEPTH, D_MODEL, IN_COLS), D_MODEL ** -0.5),
        "g_q_a": gain(ks[8], (DEPTH, Q_RANK)),
        "w_q_b": nrm(ks[9], (DEPTH, Q_RANK, N_HEADS * (QK_NOPE + QK_ROPE)), Q_RANK ** -0.5),
        "g_kv_a": gain(ks[10], (DEPTH, KV_RANK)),
        "w_kv_b": nrm(ks[11], (DEPTH, KV_RANK, N_HEADS * (QK_NOPE + V_DIM)), KV_RANK ** -0.5),
        "conv_w": nrm(ks[12], (DEPTH, 3, CONV_W), 3 ** -0.5),
        "conv_b": nrm(ks[13], (DEPTH, CONV_W), 0.01),
        "g_mix_out": gain(ks[14], (DEPTH, MIX_W)),
        "w_out": nrm(ks[15], (DEPTH, MIX_W, D_MODEL), MIX_W ** -0.5),
        "g_ffn_norm": gain(ks[16], (DEPTH, D_MODEL)),
        "w_up": nrm(ks[17], (DEPTH, D_MODEL, 2 * FFN_DIM), D_MODEL ** -0.5),
        "ffn_conv_w": nrm(ks[18], (DEPTH, 3, 2 * FFN_DIM), 3 ** -0.5),
        "ffn_conv_b": nrm(ks[19], (DEPTH, 2 * FFN_DIM), 0.01),
        "w_down": nrm(ks[20], (DEPTH, FFN_DIM, D_MODEL), FFN_DIM ** -0.5),
        "g_final": gain(ks[21], (D_MODEL,)),
    }

def first_block(x, c, ctx, c_ctx, w_ada, b_ada, g_mix_norm, w_in, g_q_a, w_q_b, g_kv_a, w_kv_b,
              conv_w, conv_b, g_mix_out, w_out, g_ffn_norm, w_up, ffn_conv_w, ffn_conv_b,
              w_down, g_final):
    n_tok = x.shape[1]
    rope_lat = axial_rope_tables(n_tok, x.dtype)
    xc = ctx
    for l in range(DEPTH):
        last = l == DEPTH - 1
        mod_l = (jax.nn.silu(c) @ w_ada[l] + b_ada[l])[:, None, :]
        mod_c = (jax.nn.silu(c_ctx) @ w_ada[l] + b_ada[l])[None, None, :]
        sh_a, sc_a, gt_a, sh_f, sc_f, gt_f = jnp.split(mod_l, 6, axis=-1)
        csh_a, csc_a, cgt_a, csh_f, csc_f, cgt_f = jnp.split(mod_c, 6, axis=-1)

        h_l = modulate(rms_norm(x, g_mix_norm[l]), sh_a, sc_a)
        h_c = modulate(rms_norm(xc, g_mix_norm[l]), csh_a, csc_a)
        qa_l, kva_l, kr_l, cb_l, cc_l, ch_l = split_projection(h_l @ w_in[l])
        qa_c, kva_c, kr_c, cb_c, cc_c, ch_c = split_projection(h_c @ w_in[l])

        k_l, v_l = mla_key_value(kva_l, kr_l, g_kv_a[l], w_kv_b[l], rope_lat)
        k_c, v_c = mla_key_value(kva_c, kr_c, g_kv_a[l], w_kv_b[l], None)
        q_l = mla_query(qa_l, g_q_a[l], w_q_b[l], rope_lat)
        att_l = block_attention(q_l, jnp.concatenate([k_l, k_c], axis=2),
                                jnp.concatenate([v_l, v_c], axis=2))
        conv_l = short_conv(cb_l, cc_l, ch_l, conv_w[l], conv_b[l])
        x = x + gt_a * merge_heads(att_l, conv_l, g_mix_out[l], w_out[l])

        if not last:
            q_c = mla_query(qa_c, g_q_a[l], w_q_b[l], None)
            att_c = block_attention(q_c, k_c, v_c)
            conv_c = short_conv(cb_c, cc_c, ch_c, conv_w[l], conv_b[l])
            xc = xc + cgt_a * merge_heads(att_c, conv_c, g_mix_out[l], w_out[l])
            hf_c = modulate(rms_norm(xc, g_ffn_norm[l]), csh_f, csc_f)
            xc = xc + cgt_f * conv_ffn(hf_c, w_up[l], ffn_conv_w[l], ffn_conv_b[l], w_down[l])

        hf_l = modulate(rms_norm(x, g_ffn_norm[l]), sh_f, sc_f)
        x = x + gt_f * conv_ffn(hf_l, w_up[l], ffn_conv_w[l], ffn_conv_b[l], w_down[l])
    return rms_norm(x, g_final)


DEPTH_2 = 2

HEAD_DIM = 128
N_HEADS_A = D_MODEL // HEAD_DIM
N_KV_A = 4
ROT_DIM = HEAD_DIM // 4
IDX_HEADS = 16
IDX_DIM = 64
IDX_ROT = IDX_DIM // 4
TOPK_MAX = 256
N_HEADS_B = D_MODEL // HEAD_DIM
N_KV_B = 4
BLOCK_Q = 128
PLE_DIM = 256
ROPE_THETA = 500000.0
LN_EPS = 1e-5
N_A_LAYERS = DEPTH_2 // 2
N_B_LAYERS = DEPTH_2 - N_A_LAYERS
ALPHA = (2.0 * DEPTH_2) ** 0.25
BETA = (8.0 * DEPTH_2) ** -0.25

WIDTH_A = N_HEADS_A * HEAD_DIM
KVW_A = N_KV_A * HEAD_DIM
SPLITS_A = tuple(int(c) for c in np.cumsum([WIDTH_A, KVW_A, KVW_A, WIDTH_A, IDX_HEADS * IDX_DIM, IDX_DIM]))
COLS_A = WIDTH_A + 2 * KVW_A + WIDTH_A + IDX_HEADS * IDX_DIM + IDX_DIM + IDX_HEADS
WIDTH_B = N_HEADS_B * HEAD_DIM
KVW_B = N_KV_B * HEAD_DIM


def layer_norm(x, g, b):
    xf = x.astype(jnp.float32)
    mu = jnp.mean(xf, axis=-1, keepdims=True)
    var = jnp.mean(jnp.square(xf - mu), axis=-1, keepdims=True)
    y = (xf - mu) * lax.rsqrt(var + LN_EPS) * g.astype(jnp.float32) + b.astype(jnp.float32)
    return y.astype(x.dtype)

def partial_rope(x, positions, rot_dim):
    half = rot_dim // 2
    inv = 1.0 / (ROPE_THETA ** (jnp.arange(half, dtype=jnp.float32) / half))
    ang = positions.astype(jnp.float32)[..., None] * inv
    cos = jnp.cos(ang)[:, :, None, :]
    sin = jnp.sin(ang)[:, :, None, :]
    xr = x[..., :rot_dim].astype(jnp.float32)
    x1, x2 = xr[..., :half], xr[..., half:]
    rot = jnp.concatenate([x1 * cos - x2 * sin, x1 * sin + x2 * cos], axis=-1)
    return jnp.concatenate([rot.astype(x.dtype), x[..., rot_dim:]], axis=-1)

def to_blocks(a):
    b, s = a.shape[0], a.shape[1]
    return jnp.swapaxes(a.reshape((b, s // BLOCK_Q, BLOCK_Q) + a.shape[2:]), 0, 1)

def from_blocks(a):
    a = jnp.swapaxes(a, 0, 1)
    return a.reshape((a.shape[0], a.shape[1] * a.shape[2]) + a.shape[3:])

def mixer_a(x, w_in, w_o, positions):
    b, s, _ = x.shape
    proj = x @ w_in
    q, k, v, gate, iq, ik, iw = jnp.split(proj, SPLITS_A, axis=-1)
    q = partial_rope(q.reshape(b, s, N_HEADS_A, HEAD_DIM), positions, ROT_DIM)
    k = partial_rope(k.reshape(b, s, N_KV_A, HEAD_DIM), positions, ROT_DIM)
    v = v.reshape(b, s, N_KV_A, HEAD_DIM)
    iq = partial_rope(iq.reshape(b, s, IDX_HEADS, IDX_DIM), positions, IDX_ROT)
    ik = partial_rope(ik.reshape(b, s, 1, IDX_DIM), positions, IDX_ROT)[:, :, 0, :]
    n_sel = min(TOPK_MAX, s // 4)
    groups = N_HEADS_A // N_KV_A
    key_pos = jnp.arange(s, dtype=jnp.int32)
    idx_scale = (IDX_DIM ** -0.5) * (IDX_HEADS ** -0.5)
    starts = jnp.arange(s // BLOCK_Q, dtype=jnp.int32) * BLOCK_Q

    def block_fn(args):
        qb, iqb, iwb, start = args
        t = start + jnp.arange(BLOCK_Q, dtype=jnp.int32)
        dots = jnp.einsum('bqhd,bsd->bqhs', iqb, ik).astype(jnp.float32)
        iscore = jnp.einsum('bqhs,bqh->bqs', jax.nn.relu(dots), iwb.astype(jnp.float32)) * idx_scale
        causal = key_pos[None, :] <= t[:, None]
        iscore = jnp.where(causal[None], iscore, -jnp.inf)
        _, idx = lax.top_k(iscore, n_sel)
        ksel = jax.vmap(lambda kk, ii: kk[ii])(k, idx)
        vsel = jax.vmap(lambda vv, ii: vv[ii])(v, idx)
        qg = qb.reshape(b, BLOCK_Q, N_KV_A, groups, HEAD_DIM)
        logits = jnp.einsum('bqngd,bqknd->bqngk', qg, ksel).astype(jnp.float32) * (HEAD_DIM ** -0.5)
        valid = idx <= t[None, :, None]
        logits = jnp.where(valid[:, :, None, None, :], logits, -jnp.inf)
        wts = jax.nn.softmax(logits, axis=-1).astype(v.dtype)
        o = jnp.einsum('bqngk,bqknd->bqngd', wts, vsel)
        return o.reshape(b, BLOCK_Q, WIDTH_A)

    o = from_blocks(lax.map(block_fn, (to_blocks(q), to_blocks(iq), to_blocks(iw), starts)))
    return (o * jax.nn.silu(gate)) @ w_o

def shared_kv(x, w_kv):
    b, s, _ = x.shape
    k, v = jnp.split(x @ w_kv, [KVW_B], axis=-1)
    return k.reshape(b, s, N_KV_B, HEAD_DIM), v.reshape(b, s, N_KV_B, HEAD_DIM)

def mixer_b(x, w_in, w_o, k, v):
    b, s, _ = x.shape
    q, gate = jnp.split(x @ w_in, [WIDTH_B], axis=-1)
    q = q.reshape(b, s, N_HEADS_B, HEAD_DIM)
    groups = N_HEADS_B // N_KV_B
    key_pos = jnp.arange(s, dtype=jnp.int32)
    starts = jnp.arange(s // BLOCK_Q, dtype=jnp.int32) * BLOCK_Q

    def block_fn(args):
        qb, start = args
        t = start + jnp.arange(BLOCK_Q, dtype=jnp.int32)
        qg = qb.reshape(b, BLOCK_Q, N_KV_B, groups, HEAD_DIM)
        z = jnp.einsum('bqngd,bsnd->bngqs', qg, k).astype(jnp.float32) * (HEAD_DIM ** -0.5)
        strict = key_pos[None, :] < t[:, None]
        log_om = jnp.where(strict, -jax.nn.softplus(z), 0.0)
        suffix = lax.cumsum(log_om, axis=log_om.ndim - 1, reverse=True) - log_om
        a = jnp.where(strict, jnp.exp(jax.nn.log_sigmoid(z) + suffix), 0.0)
        o = jnp.einsum('bngqs,bsnd->bqngd', a.astype(v.dtype), v)
        return o.reshape(b, BLOCK_Q, WIDTH_B)

    o = from_blocks(lax.map(block_fn, (to_blocks(q), starts)))
    return (o * jax.nn.silu(gate)) @ w_o

def per_layer_embed(x, p_i, w_p, w_g):
    return (p_i @ w_p) * jax.nn.sigmoid(x @ w_g)

def second_inputs(seed: int = 0) -> dict:
    key = jax.random.key(seed)
    ks = jax.random.split(key, 12)
    nrm = jax.random.normal
    x = nrm(ks[0], (BATCH, SEQ, D_MODEL), jnp.float32)
    p = nrm(ks[1], (DEPTH_2, BATCH, SEQ, PLE_DIM), jnp.float32)
    positions = jnp.broadcast_to(jnp.arange(SEQ, dtype=jnp.int32)[None, :], (BATCH, SEQ))
    w_in_a = nrm(ks[2], (N_A_LAYERS, D_MODEL, COLS_A), jnp.float32) * D_MODEL ** -0.5
    w_o_a = nrm(ks[3], (N_A_LAYERS, WIDTH_A, D_MODEL), jnp.float32) * (WIDTH_A ** -0.5 * BETA)
    w_kv_b = nrm(ks[4], (D_MODEL, 2 * KVW_B), jnp.float32) * D_MODEL ** -0.5
    w_in_b = nrm(ks[5], (N_B_LAYERS, D_MODEL, 2 * WIDTH_B), jnp.float32) * D_MODEL ** -0.5
    w_o_b = nrm(ks[6], (N_B_LAYERS, WIDTH_B, D_MODEL), jnp.float32) * (WIDTH_B ** -0.5 * BETA)
    ln_g = 1.0 + 0.02 * nrm(ks[7], (DEPTH_2, D_MODEL), jnp.float32)
    ln_b = 0.02 * nrm(ks[8], (DEPTH_2, D_MODEL), jnp.float32)
    w_ple = nrm(ks[9], (DEPTH_2, PLE_DIM, D_MODEL), jnp.float32) * PLE_DIM ** -0.5
    w_ple_gate = nrm(ks[10], (DEPTH_2, D_MODEL, D_MODEL), jnp.float32) * D_MODEL ** -0.5
    return {"x": x, "p": p, "positions": positions, "w_in_a": w_in_a, "w_o_a": w_o_a,
            "w_kv_b": w_kv_b, "w_in_b": w_in_b, "w_o_b": w_o_b, "ln_g": ln_g, "ln_b": ln_b,
            "w_ple": w_ple, "w_ple_gate": w_ple_gate}

def second_block(x, p, positions, w_in_a, w_o_a, w_kv_b, w_in_b, w_o_b, ln_g, ln_b, w_ple, w_ple_gate):
    k_sh, v_sh = None, None
    for i in range(DEPTH_2):
        if i < N_A_LAYERS:
            h = mixer_a(x, w_in_a[i], w_o_a[i], positions)
        else:
            if i == N_A_LAYERS:
                k_sh, v_sh = shared_kv(x, w_kv_b)
            j = i - N_A_LAYERS
            h = mixer_b(x, w_in_b[j], w_o_b[j], k_sh, v_sh)
        x = layer_norm(ALPHA * x + h, ln_g[i], ln_b[i])
        x = x + per_layer_embed(x, p[i], w_ple[i], w_ple_gate[i])
    return x


def setup_inputs(seed=0):
    out = dict(first_inputs(seed))
    for name, value in second_inputs(seed + 1).items():
        if name != "x":
            out[name + "_2"] = value
    return out


def reference(
    x, c, ctx, c_ctx, w_ada, b_ada, g_mix_norm, w_in, g_q_a, w_q_b, g_kv_a, w_kv_b, conv_w,
    conv_b, g_mix_out, w_out, g_ffn_norm, w_up, ffn_conv_w, ffn_conv_b, w_down, g_final, p_2,
    positions_2, w_in_a_2, w_o_a_2, w_kv_b_2, w_in_b_2, w_o_b_2, ln_g_2, ln_b_2, w_ple_2,
    w_ple_gate_2,
):
    x = first_block(
        x, c, ctx, c_ctx, w_ada, b_ada, g_mix_norm, w_in, g_q_a, w_q_b, g_kv_a, w_kv_b, conv_w,
        conv_b, g_mix_out, w_out, g_ffn_norm, w_up, ffn_conv_w, ffn_conv_b, w_down, g_final,
    )
    return second_block(
        x, p_2, positions_2, w_in_a_2, w_o_a_2, w_kv_b_2, w_in_b_2, w_o_b_2, ln_g_2, ln_b_2,
        w_ple_2, w_ple_gate_2,
    )


_drawn_inputs = setup_inputs


def setup_inputs(seed=0):
    import zlib

    import numpy as np

    out = dict(_drawn_inputs(seed))
    spreads = {}
    factors = {'b_ada': 3.409,
     'g_mix_norm': 4.913,
     'g_q_a': 8.0,
     'g_kv_a': 6.111,
     'conv_b': 8.0,
     'g_mix_out': 5.48,
     'g_ffn_norm': 5.134,
     'ffn_conv_b': 8.0,
     'g_final': 3.222}
    for name, (base, spread) in spreads.items():
        noise = np.random.default_rng([zlib.crc32(name.encode()), seed]).standard_normal(out[name].shape)
        drawn = base * np.exp(spread * noise) if base else spread * noise
        out[name] = __import__('jax').numpy.asarray(drawn.astype(out[name].dtype))
    for name, factor in factors.items():
        out[name] = (out[name] * factor).astype(out[name].dtype)
    return out
```

```python
import numpy as np

P = 128
T = 256
D = 2048
KD = D // P
CHUNK = 2048

NH1, NOPE, ROPE, VD = 8, 128, 64, 128
Q_RANK, KV_RANK, CONV_W = 512, 256, 1024
FFN = 5504
FT = FFN // P
PARTS = ((0, 16), (16, 32), (32, FT))
EPS, LN_EPS = 1e-6, 1e-5
NH2, NKV, HD = 16, 4, 128
IH, ID = 16, 64
TOPK = 64
THETA = 500000.0
ALPHA = 4.0 ** 0.25
NEG, MARK, BIG = -3.0e38, -3.4e38, 1.0e30

VEC = {}
_at = 0
for _name, _n in (("c", KD), ("c_ctx", KD), ("b_ada", 6 * KD), ("g_mix_norm", KD), ("g_q_a", 4), ("g_kv_a", 2),
                  ("conv", 8 * 4), ("g_mix_out", KD), ("g_ffn_norm", KD), ("ffn_conv", (FT + 1) // 2 * 16), ("g_final", KD),
                  ("ln_g", 2 * KD), ("ln_b", 2 * KD)):
    VEC[_name] = (_at, _n)
    _at += _n
NVEC = _at
CON = {}
_at = 0
for _name, _n in (("ident", P), ("rot1", P), ("cos1", T), ("sin1", T), ("inv2", 1), ("invi", 1), ("half_pi", 1),
                  ("rot2", P), ("roti", P), ("tri", P), ("strict", P)):
    CON[_name] = (_at, _n)
    _at += _n
NCON = _at
NCON1 = CON["rot2"][0]


def schedule():
    chunks, phases = [], {}
    groups = [0]

    def phase(name):
        phases[name] = (len(chunks), groups[0])

    def group(key, cols, ks=range(KD), per=4, layer=0, n_groups=1):
        ks = list(ks)
        for j in range(0, len(ks), per):
            chunks.append((key, layer, ks[j:j + per], cols))
        groups[0] += n_groups

    def wide(name, key, first, n, layer=0):
        phase(name)
        for g in range(n):
            group(key, [(first + 512 * g, first + 512 * (g + 1))], layer=layer)

    kr = (Q_RANK + KV_RANK, Q_RANK + KV_RANK + ROPE)
    phase("kv_in")
    group("w_in", [(Q_RANK, Q_RANK + KV_RANK), kr, kr])
    phase("q_in")
    group("w_in", [(0, Q_RANK)])
    wide("conv_in", "w_in", kr[1], 6)
    phase("q_b")
    hw = NOPE + ROPE
    for h in range(0, NH1, 2):
        nope = [(hw * i, hw * i + NOPE) for i in (h, h + 1)]
        rope = [(hw * i + NOPE, hw * (i + 1)) for i in (h, h + 1)]
        group("w_q_b", nope + rope, range(4))
    phase("kv_b")
    group("w_kv_b", [(256 * h, 256 * h + NOPE) for h in range(NH1)], range(2), n_groups=4)
    group("w_kv_b", [(256 * h + NOPE, 256 * (h + 1)) for h in range(NH1)], range(2), n_groups=4)
    phase("att1")
    groups[0] += NH1
    wide("w_out", "w_out", 0, 4)
    for n, (a, b) in enumerate(PARTS):
        phase(f"up{n}")
        for f in range(a, b, 2):
            w = P * min(2, b - f)
            group("w_up", [(P * f, P * f + w), (FFN + P * f, FFN + P * f + w)], per=CHUNK // (2 * w))
        phase(f"down{n}")
        for g in range(4):
            group("w_down", [(512 * g, 512 * (g + 1))], range(a, b))
    phase("ikw")
    group("w_in_a_2", [(6144, 6208), (6144, 6208), (6208, 6224)], per=8)
    wide("iq", "w_in_a_2", 5120, 2)
    phase("index")
    wide("k_a", "w_in_a_2", 2048, 1)
    wide("v_a", "w_in_a_2", 2560, 1)
    wide("q_a", "w_in_a_2", 0, 4)
    wide("gate_a", "w_in_a_2", 3072, 4)
    phase("att2")
    groups[0] += NH2
    wide("o_a", "w_o_a_2", 0, 4)

    def embed(i):
        wide(f"pgate{i}", "w_ple_gate_2", 0, 4, layer=i)
        phase(f"ple{i}")
        for g in range(2):
            group("w_ple_2", [(1024 * g, 1024 * (g + 1))], range(2), layer=i, n_groups=2)

    embed(0)
    wide("k_b", "w_kv_b_2", 0, 1)
    wide("v_b", "w_kv_b_2", 512, 1)
    wide("q_bb", "w_in_b_2", 0, 4)
    wide("gate_b", "w_in_b_2", D, 4)
    phase("att3")
    groups[0] += NH2
    wide("o_b", "w_o_b_2", 0, 4)
    embed(1)
    while len(chunks) % 4:
        chunks.append(None)
    return chunks, phases


def two_blocks(nc, stream, ada_stream, vecs, consts, x_t, ctx_t, p_t, positions, out):
    import concourse.bass as bass
    from concourse import mybir

    F32, F32R, I32 = mybir.dt.float32, mybir.dt.float32r, mybir.dt.int32
    ALU, ACT, AX = mybir.AluOpType, mybir.ActivationFunctionType, mybir.AxisListType
    chunks, PH = schedule()
    N_CHUNKS = len(chunks)
    WK = T * KD * 4

    at = [nc.sbuf_base + (-nc.sbuf_base) % 64]

    def place(name, shape, dt=F32, offset=None):
        size = int(np.prod(shape[1:])) * 4
        if offset is None:
            offset = at[0]
            at[0] += size + (-size) % 32
        return nc.alloc_sbuf_tensor_at(name, shape, dt, offset=offset)

    RAW = [place(f"raw{i}", [P, CHUNK]) for i in range(4)]
    HI = [place(f"hi{i}", [P, CHUNK], F32R) for i in range(2)]
    LO = [place(f"lo{i}", [P, CHUNK], F32R) for i in range(2)]
    X = place("x", [P, KD, T])
    o_ada = at[0]
    ADA = [place(f"ada_raw{i}", [P, CHUNK]) for i in range(2)]
    FMA = [place(f"ada_acc{i}", [P, 2, 512]) for i in range(2)]
    oA = at[0]; at[0] += WK
    oB = at[0]; at[0] += WK
    oY = at[0]; at[0] += WK
    oU = at[0]; at[0] += 2 * WK
    AH, AL = place("act_hi", [P, KD, T], F32R, oA), place("act_lo", [P, KD, T], F32R, oB)
    QT1 = place("q1", [P, 12, T], F32, oA)
    V1 = place("v1", [P, 4, 1024], F32, oB)
    SQC = place("ctx_squares", [P, KD, T], F32, oA)
    Y = place("y", [P, KD, T], F32, oY)
    KVH, KVL = place("kv_hi", [P, 2, 512], F32R, oY), place("kv_lo", [P, 2, 512], F32R, oY + 4096)
    QH, QL = place("qa_hi", [P, 4, T], F32R, oY + 8192), place("qa_lo", [P, 4, T], F32R, oY + 12288)
    U = place("u", [P, 2 * KD, T], F32, oU)
    UH, UL = place("u_hi", [P, KD, T], F32R, oU), place("u_lo", [P, KD, T], F32R, oU + WK)
    CTX = place("ctx", [P, KD, T], F32, oU + WK)
    FMA += [place(f"ada_acc{i}", [P, 2, 512], F32, oU + 4096 * (i - 2)) for i in (2, 3)]
    KN1 = place("k_nope1", [P, NH1, 512], F32, oU + WK)
    R0 = place("r0", [P, 1024]); R1 = place("r1", [P, 1024]); R2 = place("r2", [P, 1024])
    KR = place("k_rope", [P, 512])
    CV = place("consts", [P, NCON1])
    VV = place("vectors", [P, NVEC])
    ONES = place("ones", [P, P])
    RSTD = place("rstd", [P, 512])
    SC = place("silu_c", [P, 2 * KD])
    MOD = place("ada", [P, 6 * KD])
    MODC = place("ada_ctx", [P, 2 * KD])
    SCL = place("scales", [P, 2 * KD])
    COL = place("columns", [P, 64])
    assert at[0] <= nc.sbuf_usable_end, (at[0], nc.sbuf_usable_end)
    o2 = [o_ada]

    def later(name, shape, dt=F32):
        t = place(name, shape, dt, o2[0])
        o2[0] += int(np.prod(shape[1:])) * 4
        return t

    PTH, PTL = later("p_hi", [P, 4, T], F32R), later("p_lo", [P, 4, T], F32R)
    COS2, SIN2, COSI, SINI = (later(n, [P, T]) for n in ("cos2", "sin2", "cosi", "sini"))
    BIASM = later("topk_bias", [P, 2, T])
    IW = later("index_weights", [P, 2, IH])
    PRAW = later("p_raw", [P, 4, T])
    ZS = [place(f"z{i}", [P, 512], F32, o2[0] - 4096 + 2048 * i)[:, :] for i in range(2)]
    MINUS = later("minus_ones", [P, P])
    CV2 = later("consts2", [P, NCON - NCON1])
    POS = later("positions", [P, T], I32)
    assert o2[0] <= oA
    PT2 = [R2[:, 512 * i:512 * i + 512].rearrange("p (k q) -> p k q", k=2) for i in range(2)]
    PB = [place(f"probs{i}", [P, 512], F32, oY + 8 * 1024 + 2048 * i) for i in range(2)]
    PT = [place(f"probs_t{i}", [P, 4, T], F32, oU + 8 * 1024 + 4096 * i) for i in range(2)]

    def vec(name, i=0, n=1):
        a = VEC[name][0] + i
        return VV[:, a:a + n]

    def con(name):
        a, n = CON[name]
        return CV[:, a:a + n] if a < NCON1 else CV2[:, a - NCON1:a - NCON1 + n]

    IDENT = con("ident")
    ACC = [nc.alloc_psum_tensor(f"acc{i}", [P, 4, T], F32) for i in range(2)]
    AUX = nc.alloc_psum_tensor("aux", [P, 4, 512], F32)

    sems = {}

    def sem(name):
        if name not in sems:
            sems[name] = nc.alloc_semaphore(name)
        return sems[name]

    NORMS = {"nx": (2, 4), "nc": (2, 4), "nkv": (1, 1), "nq": (1, 1), "nf": (2, 4), "n2": (2, 4), "ln0": (2, 4),
             "ln1": (2, 4)}

    def step(name):
        norm, _, kind = name.rpartition("_")
        of = {"sq": 0, "full": 1, "hi": 1}
        if norm not in NORMS or kind not in ("sq", "ss", "tot", "var", "std", "full", "hi"):
            return sem(name), 0
        before = 0
        for other, counts in NORMS.items():
            if other == norm:
                break
            before += counts[of[kind]] if kind in of else 1
        return sem("norm_" + kind), before

    def since(name, n):
        s, before = step(name)
        return s, before + n

    raw_full = [sem(f"raw_full{i}") for i in range(4)]
    hi_done, lo_done, pe_chunk = sem("hi_done"), sem("lo_done"), sem("pe_chunk")
    acc_full, acc_free = sem("acc_full"), sem("acc_free")
    ada_full = [sem(f"ada_full{i}") for i in range(2)]
    ada_fma, ada_sum, ada_out = sem("ada_fma"), sem("ada_sum"), sem("ada_out")
    GTL = 8
    C0_FMAS = 2 * 16 * GTL

    CARRY = {"kv_in": (8, 4), "q_in": (9, 4), "conv_in": (10, 4), "w_out": (16, 4), "up0": (20, 2)}

    with nc.Block() as block:

        @block.sync
        def _(eng):
            eng.dma_start(VV[:, :], vecs).then_inc(sem("vectors_loaded"), 16)
            eng.dma_start(X[:, :, :], x_t).then_inc(sem("x_loaded"), 16)
            eng.dma_start(CTX[:, :, :], ctx_t).then_inc(sem("ctx_loaded"), 16)
            eng.dma_start(CV[:, :], consts[:, 0:NCON1]).then_inc(sem("consts_loaded"), 16)
            for c in range(4):
                eng.dma_start(RAW[c][:, :], stream[c]).then_inc(raw_full[c], 16)
            fours = stream.rearrange("(i j) p n -> j i p n", j=4)
            with eng.Fori(1, N_CHUNKS // 4) as i:
                for j in range(4):
                    eng.wait_ge(lo_done, i * 4 + (j - 3))
                    eng.dma_start(RAW[j][:, :], fours[j, bass.ds(i, 1)].rearrange("o p n -> (o p) n"))\
                       .then_inc(raw_full[j], 16)
            eng.wait_ge(sem("result"), 1)
            eng.dma_start(out, X[:, :, :]).then_inc(sem("stored"), 16)
            eng.wait_ge(sem("stored"), 16)
            for c in range(4):
                eng.wait_ge(raw_full[c], 16 * (N_CHUNKS // 4))

        @block.gpsimd
        def _(eng):
            eng.memset(ONES[:, :], 1.0).then_inc(sem("ones"), 1)

            twos = ada_stream.rearrange("(i j) p n -> j i p n", j=2)

            def load(i, slot, after):
                if after is not None:
                    eng.wait_ge(ada_fma, after)
                eng.dma_start(ADA[slot][:, :], twos[slot, bass.ds(i, 1)].rearrange("o p n -> (o p) n"))\
                   .then_inc(ada_full[slot], 16)

            load(0, 0, None)
            load(0, 1, None)
            with eng.Fori(1, 2 * GTL) as i:
                for j in range(2):
                    load(i, j, i * 16 + 8 * (j - 1))
            load(2 * GTL, 0, 8 * (4 * GTL - 1))
            load(2 * GTL, 1, 8 * 4 * GTL)
            with eng.Fori(2 * GTL + 1, 2 * 24) as i:
                for j in range(2):
                    load(i, j, i * 8 + (4 * (j - 1) + C0_FMAS // 2))

            eng.wait_ge(ada_out, 2 * GTL + 16)
            eng.dma_start(PRAW[:, :, :].rearrange("p k t -> p (k t)"), p_t).then_inc(sem("p_loaded"), 16)
            eng.dma_start(POS[:, :], positions).then_inc(sem("positions_loaded"), 16)
            eng.dma_start(CV2[:, :], consts[:, NCON1:NCON]).then_inc(sem("consts2_loaded"), 16)
            eng.memset(MINUS[:, :], -1.0).then_inc(sem("minus_ones"), 1)

            for qt in range(2):
                causal = dict(pattern=[[-1, T]], base=P * qt, channel_multiplier=1, compare_op=ALU.is_ge)
                eng.wait_ge(sem("index_scored"), qt + 1)
                a = Y[:, 13 + qt, :]
                eng.affine_select(out=a, in_=a, fill=NEG, **causal).then_inc(sem("index_masked"), 1)
            for qt in range(2):
                causal = dict(pattern=[[-1, T]], base=P * qt, channel_multiplier=1, compare_op=ALU.is_ge)
                eng.wait_ge(sem("chosen"), qt + 1)
                a = BIASM[:, qt, :]
                eng.affine_select(out=a, in_=a, fill=0.0, **causal).then_inc(sem("chosen_masked"), 1)

        @block.scalar
        def _(act):
            def split(c, base=None, reg=None, step=0):
                n = c if reg is None else c + reg * step
                act.wait_ge(raw_full[c % 4], 16 * (c // 4 + 1) if reg is None else reg * (4 * step) + 16 * (c // 4 + 1))
                if c >= 2:
                    act.wait_ge(pe_chunk, n - 1)
                nc.scalar.activation(HI[c % 2][:, :], RAW[c % 4][:, :], ACT.Copy).then_inc(hi_done, 1)

            pending = [lambda: None]

            def phase(name, n, evac=None, then=None):
                c0, g0 = PH[name]
                evac = evac or (lambda g, reg=None: None)

                def pair(first, reg=None):
                    c = c0 + (0 if first else 8)
                    ri = None if reg is None else reg - 1
                    for j in range(8):
                        split(c + j, reg=ri, step=8)
                        if j == 1:
                            if first:
                                pending[0]()
                            else:
                                evac(1, reg - 1)
                        if j == 5:
                            evac(0, 0 if first else reg)
                if n == 1:
                    for j in range(4):
                        split(c0 + j)
                        if j == 1:
                            pending[0]()
                    last = (0, 0)
                else:
                    pair(True)
                    if n > 3:
                        with act.Fori(1, n // 2) as i:
                            pair(False, i)
                    last = (1, n // 2 - 1)
                    if n % 2:
                        for j in range(4):
                            split(c0 + 4 * (n - 1) + j)
                            if j == 1:
                                evac(*last)
                        last = (0, n // 2)

                def rest():
                    evac(*last)
                    if then:
                        then()
                pending[0] = rest

            def flush():
                pending[0]()
                pending[0] = lambda: None

            def hi_of(src, dst, ready, done, parts=4, n=4):
                for q in range(parts):
                    act.wait_ge(*since(ready, q + 1))
                    nc.scalar.activation(dst[:, n * q:n * q + n, :], src[:, n * q:n * q + n, :], ACT.Copy)\
                        .then_inc(step(done)[0], 1)

            def squares(name, src, dst, halves=2):
                n = src.shape[1] // halves
                for q in range(halves):
                    nc.scalar.activation(dst[:, n * q:n * q + n, :], src[:, n * q:n * q + n, :], ACT.Square)\
                        .then_inc(step(name + "_sq")[0], 1)

            def root(name, w):
                act.wait_ge(*since(name + "_var", 1))
                nc.scalar.activation(RSTD[:, 0:w], RSTD[:, 0:w], ACT.Sqrt).then_inc(step(name + "_std")[0], 1)

            act.wait_ge(sem("vectors_loaded"), 16)
            nc.scalar.activation(SC[:, :], vec("c", 0, 2 * KD), ACT.Silu).then_inc(sem("silu_c"), 1)
            act.wait_ge(sem("x_loaded"), 16)
            squares("nx", X, Y)
            act.wait_ge(sem("ctx_loaded"), 16)
            squares("nc", CTX, SQC)
            root("nx", T)
            root("nc", T)

            def enter():
                hi_of(Y, AH, "nx_full", "nx_hi")
                hi_of(CTX, UH, "nc_full", "nc_hi")
            pending[0] = enter
            phase("kv_in", 1, then=None)
            phase("q_in", 1, evac=None)

            def kv_norm_1():
                act.wait_ge(sem("kva"), 1)
                nc.scalar.activation(R2[:, :], R0[:, :], ACT.Square).then_inc(step("nkv_sq")[0], 1)
                root("nkv", 512)
                act.wait_ge(*since("nkv_full", 1))
                nc.scalar.activation(KVH[:, :, :], R0[:, :].rearrange("p (k t) -> p k t", k=2), ACT.Copy)\
                    .then_inc(step("nkv_hi")[0], 1)

            def q_norm_1():
                act.wait_ge(sem("qa"), 1)
                nc.scalar.activation(R2[:, :], R1[:, :], ACT.Square).then_inc(step("nq_sq")[0], 1)
                root("nq", T)
                act.wait_ge(*since("nq_full", 1))
                nc.scalar.activation(QH[:, :, :], R1[:, :].rearrange("p (k t) -> p k t", k=4), ACT.Copy)\
                    .then_inc(step("nq_hi")[0], 1)
            pending[0] = lambda: (kv_norm_1(), q_norm_1())
            phase("conv_in", 6)
            c0 = PH["q_b"][0]
            for j in range(6):
                split(c0 + j)
                if j == 1:
                    flush()
            c0 = PH["w_out"][0]

            scale1 = float(NOPE + ROPE) ** -0.5
            for u in range(2 * NH1):
                act.wait_ge(sem("max1"), u + 1)
                if u >= 2:
                    act.wait_ge(sem("turned1"), u - 1)
                nc.scalar.activation(PB[u % 2][:, :], AUX[:, u % 2, :], ACT.Exp, bias=COL[:, u % 2:u % 2 + 1],
                                     scale=scale1, accum_out=COL[:, 2 + u % 2:3 + u % 2]).then_inc(sem("exp1"), 1)
                act.wait_ge(sem("turned1"), u + 1)
                if u >= 4:
                    act.wait_ge(acc_full, PH["att1"][1] + u // 2 - 1)
                nc.scalar.activation(PT[u // 2 % 2][:, :, P * (u % 2):P * (u % 2) + P],
                                     AUX[:, 2 + u % 2, :].rearrange("p (k q) -> p k q", k=4), ACT.Copy)\
                    .then_inc(sem("probs1"), 1)

            def merge():
                src = [Y[:, 0:4, :], Y[:, 4:8, :], U[:, 0:4, :], U[:, 4:8, :]]
                for b in range(4):
                    if b == 0:
                        act.wait_ge(sem("att1_done"), 1)
                    else:
                        act.wait_ge(sem("mix_tot"), b)
                    nc.scalar.activation(U[:, 8:12, :], src[b], ACT.Square).then_inc(sem("mix_sq"), 1)
                    act.wait_ge(sem("mix_var"), b + 1)
                    nc.scalar.activation(U[:, 12:16, :], U[:, 12:16, :], ACT.Sqrt).then_inc(sem("mix_std"), 1)
                    act.wait_ge(sem("mix_full"), b + 1)
                    nc.scalar.activation(AH[:, 4 * b:4 * b + 4, :], src[b], ACT.Copy).then_inc(sem("mix_hi"), 1)
            pending[0] = merge

            def norm(name, dst):
                act.wait_ge(*since(name + "_in", 1))
                squares(name, X, Y)
                root(name, T)
                hi_of(dst, AH, name + "_full", name + "_hi")
            phase("w_out", 4, then=lambda: norm("nf", Y))

            seen = [0]

            def up_evac(parts, base):
                def evac(g, reg, tiles=2):
                    dyn = not isinstance(reg, int)
                    gi = 2 * reg + g
                    n = base[1] + gi
                    act.wait_ge(acc_full, base[0] + gi + 1)
                    if not isinstance(n, int) or n:
                        act.wait_ge(sem("up_done"), n)
                    for t in range(2 * tiles):
                        i = t if tiles == 2 else 2 * t
                        w = gi * 16 + (VEC["ffn_conv"][0] + 16 * base[1] + 4 * i)
                        nc.scalar.activation(Y[:, i, :], ACC[(base[0] + g) % 2][:, t, :], ACT.Identity,
                                             scale=VV[:, bass.ds(w + 1, 1)], bias=VV[:, bass.ds(w + 3, 1)])\
                            .then_inc(sem("up_centre"), 1)
                    act.wait_ge(sem("up_conv"), n + 1)
                    nc.scalar.activation(Y[:, 4:4 + tiles, :], Y[:, 2:2 + tiles, :], ACT.Silu)\
                        .then_inc(sem("up_silu"), 1)
                    act.wait_ge(sem("up_prod"), n + 1)
                    nc.scalar.activation(UH[:, bass.ds(gi * 2, tiles), :], Y[:, 6:6 + tiles, :], ACT.Copy)\
                        .then_inc(sem("up_hi"), 1)
                return evac

            for n, (a, b) in enumerate(PARTS):
                ev = up_evac(n, (PH[f"up{n}"][1], a // 2))
                full = (b - a) // 2
                phase(f"up{n}", full, evac=ev)
                if (b - a) % 2:
                    for j in range(2):
                        split(PH[f"up{n}"][0] + 4 * full + j)
                    flush()
                    pending[0] = lambda ev=ev, full=full: ev(full % 2, full // 2, tiles=1)
                if n < 2:
                    phase(f"down{n}", 4)
                else:
                    c0 = PH["down2"][0]
                    for j in range(12):
                        split(c0 + j)
                        if j == 1:
                            flush()
            def enter2():
                norm("n2", X)
                act.wait_ge(sem("angles"), 1)
                for i, (cos, sin) in enumerate(((COS2, SIN2), (COSI, SINI))):
                    r = Y[:, i, :]
                    nc.scalar.activation(cos[:, :], r, ACT.Abs).then_inc(sem("abs_angle"), 1)
                    nc.scalar.activation(sin[:, :], r, ACT.Sin).then_inc(sem("tables"), 1)
                for i, cos in enumerate((COS2, COSI)):
                    act.wait_ge(sem("abs_angle"), 2)
                    nc.scalar.activation(cos[:, :], cos[:, :], ACT.Sin, bias=con("half_pi"), scale=-1.0)\
                        .then_inc(sem("tables"), 1)
            pending[0] = enter2
            c0 = PH["ikw"][0]
            for j in range(2):
                split(c0 + j)
                if j == 1:
                    flush()
            phase("iq", 2)
            flush()

            for u in range(IH):
                act.wait_ge(sem("index_dots"), u + 1)
                if u >= 2:
                    act.wait_ge(sem("index_added"), 2 * (u - 1))
                nc.scalar.activation(R2[:, 512 * (u % 2):512 * (u % 2) + 512].rearrange("p (h t) -> p h t", h=2),
                                     AUX[:, 2 * (u % 2):2 * (u % 2) + 2, 0:T], ACT.Relu,
                                     scale=(ID ** -0.5) * (IH ** -0.5)).then_inc(sem("index_relu"), 1)
            phase("k_a", 1)
            phase("v_a", 1)
            phase("q_a", 4)

            def silu_gate(tag):
                def f():
                    act.wait_ge(sem("gate_" + tag), 1)
                    nc.scalar.activation(U[:, KD:2 * KD, :], U[:, KD:2 * KD, :], ACT.Silu)\
                        .then_inc(sem("silu_" + tag), 1)
                return f
            phase("gate_a", 4, then=silu_gate("a"))
            flush()

            for h in range(NH2):
                act.wait_ge(sem("max2"), h + 1)
                for qt in range(2):
                    s = PB[h % 2][:, T * qt:T * qt + T]
                    act_i = nc.scalar.activation(s, s, ACT.Exp, bias=COL[:, 4 * (h % 2) + qt:4 * (h % 2) + qt + 1],
                                                 accum_out=COL[:, 4 * (h % 2) + 2 + qt:4 * (h % 2) + 3 + qt])
                act_i.then_inc(sem("exp2"), 1)
                act.wait_ge(sem("turned2"), h + 1)
                if h >= 2:
                    act.wait_ge(acc_full, PH["att2"][1] + h - 1)
                nc.scalar.activation(PT2[h % 2], AUX[:, 2 + h % 2, :].rearrange("p (k q) -> p k q", k=2), ACT.Copy)\
                    .then_inc(sem("probs2"), 1)

            def out_split(tag):
                def f():
                    act.wait_ge(sem("att_" + tag), 1)
                    for q in range(4):
                        nc.scalar.activation(AH[:, 4 * q:4 * q + 4, :], U[:, 4 * q:4 * q + 4, :], ACT.Copy)\
                            .then_inc(sem("att_hi_" + tag), 1)
                return f
            pending[0] = out_split("a")

            def layer_norm(i):
                def f():
                    act.wait_ge(sem(f"ln{i}_centred"), 4)
                    squares(f"ln{i}", X, Y)
                    root(f"ln{i}", T)
                    hi_of(X, AH, f"ln{i}_full", f"ln{i}_hi")
                return f

            def embed(i, then):
                def sig():
                    act.wait_ge(sem(f"pgate{i}_out"), 1)
                    nc.scalar.activation(U[:, 0:KD, :], U[:, 0:KD, :], ACT.Sigmoid).then_inc(sem(f"pgate{i}_sig"), 1)
                phase(f"pgate{i}", 4, then=sig)
                c0 = PH[f"ple{i}"][0]
                split(c0)
                split(c0 + 1)
                flush()
                pending[0] = then

            phase("o_a", 4, then=layer_norm(0))
            act.wait_ge(sem("p_loaded"), 16)
            nc.scalar.activation(PTH[:, :, :], PRAW[:, :, :], ACT.Copy).then_inc(sem("p_hi"), 1)
            embed(0, lambda: hi_of(X, AH, "x1_full", "x1_hi"))
            phase("k_b", 1)
            phase("v_b", 1)
            phase("q_bb", 4)
            phase("gate_b", 4, then=silu_gate("b"))
            flush()
            for h in range(NH2):
                z, w1 = ZS[h % 2], PB[h % 2][:, :]
                act.wait_ge(sem("z3"), h + 1)
                nc.scalar.activation(w1, z, ACT.Abs).then_inc(sem("act3"), 1)
                act.wait_ge(sem("act3"), 4 * h + 1)
                nc.scalar.activation(w1, w1, ACT.Exp, scale=-1.0).then_inc(sem("act3"), 1)
                act.wait_ge(sem("act3"), 4 * h + 2)
                nc.scalar.activation(w1, w1, ACT.Ln, bias=1.0).then_inc(sem("act3"), 1)
                act.wait_ge(sem("w3"), h + 1)
                nc.scalar.activation(w1, z, ACT.Exp).then_inc(sem("act3"), 1)
            pending[0] = out_split("b")
            phase("o_b", 4, then=layer_norm(1))
            embed(1, lambda: None)

        @block.vector
        def _(dve):
            V = nc.vector
            chain = [0]

            def link(ins):
                chain[0] += 1
                ins.then_inc(sem("dve_chain"), 1)
                dve.wait_ge(sem("dve_chain"), chain[0])

            def split(c, reg=None, step=0):
                n = c if reg is None else c + reg * step
                dve.wait_ge(hi_done, n + 1)
                if c >= 2:
                    dve.wait_ge(pe_chunk, n - 1)
                V.tensor_tensor(LO[c % 2][:, :], RAW[c % 4][:, :], HI[c % 2][:, :].bitcast(F32), ALU.subtract)\
                    .then_inc(lo_done, 1)

            def take(g):
                dve.wait_ge(acc_full, g + 1)

            def ada_chunk(ag, j, vectors, n0, slot, full, first_wait=None):
                dve.wait_ge(ada_full[slot], full)
                nv = len(vectors)
                for k in range(4):
                    for v, (col, accs) in enumerate(vectors):
                        n = n0 + nv * k + v
                        a = accs[:, k % 2, :]
                        w = ADA[slot][:, 512 * k:512 * k + 512]
                        s = SC[:, col + 4 * j + k:col + 4 * j + k + 1]
                        if j == 0 and k < 2:
                            if k == 0 and v == 0 and first_wait is not None:
                                dve.wait_ge(ada_sum, first_wait)
                            V.tensor_scalar(a, w, s, None, ALU.mult).then_inc(ada_fma, 1)
                        else:
                            dve.wait_ge(ada_fma, n - (2 * nv - 1))
                            V.scalar_tensor_tensor(out=a, in0=w, scalar=s, in1=a, op0=ALU.mult, op1=ALU.add)\
                                .then_inc(ada_fma, 1)

            def ada_take(ag, col, dst, sums):
                dve.wait_ge(ada_sum, sums)
                V.tensor_tensor(dst[:, bass.ds(ag * 4, 4)], AUX[:, 3, 8 * col:8 * col + 4],
                                VV[:, bass.ds(ag * 4 + VEC["b_ada"][0], 4)], ALU.add).then_inc(ada_out, 1)

            pending = [lambda: None]

            def carried(name, j, g, reg):
                if name not in CARRY:
                    return
                first, per = CARRY[name]
                if per == 2:
                    ag = first + (reg if reg is not None else 0)
                    jj = 2 * g + j
                    if j >= 2:
                        return
                    n0 = (ag - GTL) * 16 + (C0_FMAS + 4 * jj)
                    full = ag * 32 + 16 * (jj // 2 + 1)
                    ada_chunk(ag, jj, [(0, FMA[0])], n0, jj % 2, full,
                              first_wait=(ag - GTL) + GTL if jj == 0 else None)
                else:
                    ag = first + g + (2 * reg if reg is not None else 0)
                    n0 = (ag - GTL) * 16 + (C0_FMAS + 4 * j)
                    full = ag * 32 + 16 * (j // 2 + 1)
                    ada_chunk(ag, j, [(0, FMA[(first + g) % 2])], n0, j % 2, full,
                              first_wait=(ag - 1) if j == 0 else None)

            def carried_take(name, g, reg):
                if name not in CARRY:
                    return
                first, per = CARRY[name]
                if per == 2:
                    if g == 0:
                        return
                    ag = reg + first
                    if isinstance(reg, int):
                        ag = first + reg
                else:
                    ag = 2 * reg + (first + g)
                ada_take(ag, 0, MOD, ag + 1)

            def phase(name, n, evac, then=None):
                c0, g0 = PH[name]

                def pair(first, reg=None):
                    c = c0 + (0 if first else 8)
                    ri = None if reg is None else reg - 1
                    for j in range(8):
                        split(c + j, reg=ri, step=8)
                        carried(name, j % 4, j // 4, reg)
                        if j == 1:
                            if first:
                                pending[0]()
                            else:
                                evac(1, reg - 1)
                                carried_take(name, 1, reg - 1)
                        if j == 5:
                            evac(0, 0 if first else reg)
                            carried_take(name, 0, 0 if first else reg)
                if n == 1:
                    for j in range(4):
                        split(c0 + j)
                        carried(name, j, 0, None)
                        if j == 1:
                            pending[0]()
                    last = (0, 0)
                else:
                    pair(True)
                    if n > 3:
                        with dve.Fori(1, n // 2) as i:
                            pair(False, i)
                    last = (1, n // 2 - 1)
                    if n % 2:
                        for j in range(4):
                            split(c0 + 4 * (n - 1) + j)
                            if j == 1:
                                evac(*last)
                        last = (0, n // 2)

                def rest():
                    evac(*last)
                    carried_take(name, *last)
                    if then:
                        then()
                pending[0] = rest

            def flush():
                pending[0]()
                pending[0] = lambda: None

            def copy_out(name, dst, d0, n=4):
                g0 = PH[name][1]

                def evac(g, reg):
                    gi = 2 * reg + g
                    take(g0 + gi)
                    V.tensor_copy(dst[:, bass.ds(gi * 4 + d0, n), :], ACC[(g0 + g) % 2][:, 0:n, :])\
                        .then_inc(acc_free, 1)
                return evac

            def total(name, src, w, order="p k t -> p t k", halves=2):
                dve.wait_ge(*since(name + "_sq", halves))
                V.tensor_reduce(RSTD[:, 0:w], src.rearrange(order), AX.X, ALU.add).then_inc(step(name + "_ss")[0], 1)

            def variance(name, w, n, eps):
                dve.wait_ge(*since(name + "_tot", 1))
                V.tensor_scalar(RSTD[:, 0:w], AUX[:, 0, 0:w], 1.0 / n, eps, ALU.mult, ALU.add)\
                    .then_inc(step(name + "_var")[0], 1)
                dve.wait_ge(*since(name + "_std", 1))
                link(V.reciprocal(RSTD[:, 0:w], RSTD[:, 0:w]))

            def wide_bcast(a, n):
                return a.unsqueeze(1).to_broadcast([P, n, a.shape[-1]])

            def lo_of(src, dst_hi, dst_lo, hi_sem, parts=4, n=4, done=None):
                for q in range(parts):
                    s = slice(n * q, n * q + n)
                    dve.wait_ge(*since(hi_sem, q + 1))
                    ins = V.tensor_tensor(dst_lo[:, s, :], src[:, s, :], dst_hi[:, s, :].bitcast(F32), ALU.subtract)
                ins.then_inc(step(done)[0], 1)

            def normed(name, src, dst, scale, shift, mid=None):
                for q in range(4):
                    s = slice(4 * q, 4 * q + 4)
                    link(V.tensor_tensor(dst[:, s, :], src[:, s, :], wide_bcast(RSTD[:, 0:T], 4), ALU.mult))
                    for k in range(4 * q, 4 * q + 4):
                        ins = V.tensor_scalar(dst[:, k, :], dst[:, k, :], scale(k), None, ALU.mult) if shift is None \
                            else V.tensor_scalar(dst[:, k, :], dst[:, k, :], scale(k), shift(k), ALU.mult, ALU.add)
                    ins.then_inc(step(name + "_full")[0], 1)

            total("nx", Y[:, :, :], T)
            variance("nx", T, D, EPS)
            link(V.tensor_tensor(Y[:, :, :], X[:, :, :], wide_bcast(RSTD[:, 0:T], KD), ALU.mult))
            total("nc", SQC[:, :, :], T)
            variance("nc", T, D, EPS)
            link(V.tensor_tensor(CTX[:, :, :], CTX[:, :, :], wide_bcast(RSTD[:, 0:T], KD), ALU.mult))
            dve.wait_ge(sem("silu_c"), 1)

            def ada_pair(i, first=False):
                for par in range(2):
                    for j in range(4):
                        ag = 2 * i + par
                        ada_chunk(ag, j, [(0, FMA[par]), (KD, FMA[2 + par])], ag * 32 + 8 * j, j % 2,
                                  ag * 32 + 16 * (j // 2 + 1),
                                  first_wait=ag - 1 if j == 0 and not first else None)
                        if j == 1 and not (first and par == 0):
                            ada_take(ag - 1, 0, MOD, ag)
                            ada_take(ag - 1, 1, MODC, ag)
            ada_pair(0, True)
            with dve.Fori(1, GTL // 2) as i:
                ada_pair(i)
            ada_take(GTL - 1, 0, MOD, GTL)
            ada_take(GTL - 1, 1, MODC, GTL)
            dve.wait_ge(ada_out, 2 * GTL)
            for k, m in ((0, MOD), (KD, MODC)):
                link(V.tensor_scalar(SCL[:, k:k + KD], m[:, KD:2 * KD], 1.0, None, ALU.add))
                link(V.tensor_tensor(SCL[:, k:k + KD], SCL[:, k:k + KD], vec("g_mix_norm", 0, KD), ALU.mult))

            def enter():
                for name, a, m, s0 in (("nx", Y, MOD, 0), ("nc", CTX, MODC, KD)):
                    for k in range(KD):
                        ins = V.tensor_scalar(a[:, k, :], a[:, k, :], SCL[:, s0 + k:s0 + k + 1], m[:, k:k + 1],
                                              ALU.mult, ALU.add)
                        if k % 4 == 3:
                            ins.then_inc(step(name + "_full")[0], 1)
                lo_of(Y, AH, AL, "nx_hi", done="in_ready")
                lo_of(CTX, UH, UL, "nc_hi", done="ctx_ready")
            pending[0] = enter

            def kv_evac(g, reg):
                take(PH["kv_in"][1])
                a = R0[:, :].rearrange("p (k t) -> p k t", k=2)
                V.tensor_copy(a[:, :, 0:T], ACC[0][:, 0:2, :])
                V.tensor_copy(a[:, :, T:512], AUX[:, 0, :].rearrange("p (k t) -> p k t", k=2)).then_inc(sem("kva"), 1)
                V.tensor_copy(KR[:, T:512], AUX[:, 1, 0:T])
                V.tensor_copy(KR[:, 0:T], ACC[0][:, 2, :]).then_inc(sem("kr_copied"), 1)
                V.engine_nop().then_inc(acc_free, 1)

            def q_evac(g, reg):
                g0 = PH["q_in"][1]
                take(g0)
                V.tensor_copy(R1[:, :].rearrange("p (k t) -> p k t", k=4), ACC[g0 % 2][:, :, :])\
                    .then_inc(sem("qa"), 1)
                V.engine_nop().then_inc(acc_free, 1)

            def small_norms():
                total("nkv", R2[:, :].rearrange("p (k t) -> p k t", k=2), 512, halves=1)
                variance("nkv", 512, KV_RANK, EPS)
                for k in range(2):
                    a = R0[:, 512 * k:512 * k + 512]
                    ins = V.scalar_tensor_tensor(out=a, in0=a, scalar=vec("g_kv_a", k), in1=RSTD[:, :],
                                                 op0=ALU.mult, op1=ALU.mult)
                ins.then_inc(step("nkv_full")[0], 1)
                dve.wait_ge(*since("nkv_hi", 1))
                V.tensor_tensor(KVL[:, :, :], R0[:, :].rearrange("p (k t) -> p k t", k=2),
                                KVH[:, :, :].bitcast(F32), ALU.subtract).then_inc(sem("kv_ready"), 1)
                total("nq", R2[:, :].rearrange("p (k t) -> p k t", k=4), T, halves=1)
                variance("nq", T, Q_RANK, EPS)
                for k in range(4):
                    a = R1[:, T * k:T * k + T]
                    ins = V.scalar_tensor_tensor(out=a, in0=a, scalar=vec("g_q_a", k), in1=RSTD[:, 0:T],
                                                 op0=ALU.mult, op1=ALU.mult)
                ins.then_inc(step("nq_full")[0], 1)
                dve.wait_ge(*since("nq_hi", 1))
                V.tensor_tensor(QL[:, :, :], R1[:, :].rearrange("p (k t) -> p k t", k=4),
                                QH[:, :, :].bitcast(F32), ALU.subtract).then_inc(sem("q_ready"), 1)
                dve.wait_ge(sem("kr_rot"), 1)
                rope(KR[:, 0:T], AUX[:, 1, 0:T], con("cos1"), con("sin1"), R2[:, 0:T], R2[:, T:2 * T])

            def rope(x, rotated, cos, sin, w0, w1):
                link(V.tensor_tensor(w0, rotated, sin, ALU.mult))
                link(V.tensor_tensor(w1, x, cos, ALU.mult))
                link(V.tensor_tensor(x, w0, w1, ALU.add))

            phase("kv_in", 1, evac=kv_evac)
            phase("q_in", 1, evac=q_evac, then=small_norms)
            phase("conv_in", 6, evac=copy_out("conv_in", U, 0))

            def conv_branch():
                dve.wait_ge(acc_free, PH["q_b"][1])
                for k in range(2):
                    s = slice(8 + 4 * k, 12 + 4 * k)
                    link(V.tensor_tensor(U[:, s, :], U[:, s, :], U[:, 16 + 4 * k:20 + 4 * k, :], ALU.mult))
                w = VEC["conv"][0]
                col = lambda k, i: VV[:, w + 4 * k + i:w + 4 * k + i + 1]
                for k in range(8):
                    ins = V.tensor_scalar(U[:, 24 + k, :], U[:, 8 + k, :], col(k, 1), col(k, 3), ALU.mult, ALU.add)
                link(ins)
                for k in range(8):
                    o = U[:, 24 + k, 1:T]
                    ins = V.scalar_tensor_tensor(out=o, in0=U[:, 8 + k, 0:T - 1], scalar=col(k, 0), in1=o,
                                                 op0=ALU.mult, op1=ALU.add)
                link(ins)
                for k in range(8):
                    o = U[:, 24 + k, 0:T - 1]
                    ins = V.scalar_tensor_tensor(out=o, in0=U[:, 8 + k, 1:T], scalar=col(k, 2), in1=o,
                                                 op0=ALU.mult, op1=ALU.add)
                link(ins)
                link(V.tensor_tensor(U[:, 0:8, :], U[:, 0:8, :], U[:, 24:32, :], ALU.mult))

            c0, g0 = PH["q_b"]
            for j in range(6):
                split(c0 + j)
                if j == 1:
                    flush()
                    conv_branch()
                if 2 <= j < 4 or j == 4:
                    pair = j - 2
                    take(g0 + pair)
                    V.tensor_copy(QT1[:, 2 * pair:2 * pair + 2, :], ACC[(g0 + pair) % 2][:, 0:2, :])
                    V.tensor_copy(QT1[:, 8 + pair, :], ACC[(g0 + pair) % 2][:, 2, :]).then_inc(acc_free, 1)
            take(g0 + 3)
            V.tensor_copy(QT1[:, 6:8, :], ACC[(g0 + 3) % 2][:, 0:2, :])
            V.tensor_copy(QT1[:, 11, :], ACC[(g0 + 3) % 2][:, 2, :]).then_inc(acc_free, 1)
            V.engine_nop().then_inc(sem("qt1"), 1)
            g0 = PH["kv_b"][1]
            for i in range(4):
                take(g0 + i)
                V.tensor_copy(KN1[:, 2 * i:2 * i + 2, :].rearrange("p a b -> p (a b)"),
                              ACC[(g0 + i) % 2][:, :, :].rearrange("p a b -> p (a b)")).then_inc(acc_free, 1)
            for i in range(4):
                take(g0 + 4 + i)
                V.tensor_copy(V1[:, i, :], ACC[(g0 + i) % 2][:, :, :].rearrange("p a b -> p (a b)"))\
                    .then_inc(acc_free, 1)
            dve.wait_ge(sem("q_rot"), 1)
            rope(QT1[:, 8:12, :], AUX[:, 0:2, :].rearrange("p a (b t) -> p (a b) t", t=T),
                 wide_bcast(con("cos1"), 4), wide_bcast(con("sin1"), 4),
                 Y[:, 0:4, :], Y[:, 4:8, :])
            V.engine_nop().then_inc(sem("att1_in"), 1)

            g0 = PH["att1"][1]
            scale1 = float(NOPE + ROPE) ** -0.5

            def weighted(u):
                dve.wait_ge(sem("exp1"), u + 1)
                link(V.reciprocal(COL[:, 4 + u % 2:5 + u % 2], COL[:, 2 + u % 2:3 + u % 2]))
                V.tensor_scalar(PB[u % 2][:, :], PB[u % 2][:, :], COL[:, 4 + u % 2:5 + u % 2], None, ALU.mult)\
                    .then_inc(sem("normed1"), 1)

            def head_out(h):
                take(g0 + h)
                V.tensor_copy(Y[:, h, :], ACC[(g0 + h) % 2][:, 0, :]).then_inc(acc_free, 1)

            for u in range(2 * NH1):
                dve.wait_ge(sem("scores1"), u + 1)
                link(V.tensor_reduce(COL[:, 6 + u % 2:7 + u % 2], AUX[:, u % 2, :], AX.X, ALU.max))
                V.tensor_scalar(COL[:, u % 2:u % 2 + 1], COL[:, 6 + u % 2:7 + u % 2], -scale1, None, ALU.mult)\
                    .then_inc(sem("max1"), 1)
                if u:
                    weighted(u - 1)
                if u % 2 and u >= 3:
                    head_out(u // 2 - 1)
            weighted(2 * NH1 - 1)
            head_out(NH1 - 1)
            V.engine_nop().then_inc(sem("att1_done"), 1)

            def merge():
                src = [Y[:, 0:4, :], Y[:, 4:8, :], U[:, 0:4, :], U[:, 4:8, :]]
                for b in range(4):
                    dve.wait_ge(sem("mix_tot"), b + 1)
                    a = 0 if b % 2 == 0 else 2
                    V.tensor_scalar(U[:, 12:16, :].rearrange("p a b -> p (a b)"),
                                    AUX[:, a:a + 2, :].rearrange("p a b -> p (a b)"), 1.0 / P, EPS,
                                    ALU.mult, ALU.add).then_inc(sem("mix_var"), 1)
                    dve.wait_ge(sem("mix_std"), b + 1)
                    link(V.reciprocal(U[:, 12:16, :], U[:, 12:16, :]))
                    for k in range(4):
                        ins = V.scalar_tensor_tensor(out=src[b][:, k, :], in0=src[b][:, k, :],
                                                     scalar=vec("g_mix_out", 4 * b + k), in1=U[:, 12 + k, :],
                                                     op0=ALU.mult, op1=ALU.mult)
                    ins.then_inc(sem("mix_full"), 1)
                    dve.wait_ge(sem("mix_hi"), b + 1)
                    ins = V.tensor_tensor(AL[:, 4 * b:4 * b + 4, :], src[b],
                                          AH[:, 4 * b:4 * b + 4, :].bitcast(F32), ALU.subtract)
                ins.then_inc(sem("mix_ready"), 1)
            pending[0] = merge

            def residual(name, gate):
                g0 = PH[name][1]

                def evac(g, reg):
                    gi = 2 * reg + g
                    take(g0 + gi)
                    for t in range(4):
                        x = X[:, bass.ds(gi * 4 + t, 1), :].rearrange("p a t -> p (a t)")
                        ins = V.scalar_tensor_tensor(out=x, in0=ACC[(g0 + g) % 2][:, t, :],
                                                     scalar=MOD[:, bass.ds(gi * 4 + (gate + t), 1)], in1=x,
                                                     op0=ALU.mult, op1=ALU.add)
                    ins.then_inc(acc_free, 1)
                return evac

            def ffn_in():
                g_end = PH["up0"][1]
                dve.wait_ge(acc_free, g_end)
                V.engine_nop().then_inc(sem("nf_in"), 1)
                dve.wait_ge(ada_out, 2 * GTL + 12)
                link(V.tensor_scalar(SCL[:, 0:KD], MOD[:, 4 * KD:5 * KD], 1.0, None, ALU.add))
                link(V.tensor_tensor(SCL[:, 0:KD], SCL[:, 0:KD], vec("g_ffn_norm", 0, KD), ALU.mult))
                total("nf", Y[:, :, :], T)
                variance("nf", T, D, EPS)
                normed("nf", X, Y, lambda k: SCL[:, k:k + 1], lambda k: MOD[:, 3 * KD + k:3 * KD + k + 1])
                lo_of(Y, AH, AL, "nf_hi", done="ffn_ready")
            phase("w_out", 4, evac=residual("w_out", 2 * KD), then=ffn_in)

            def up_evac(base):
                def evac(g, reg, tiles=2):
                    gi = 2 * reg + g
                    n = base[1] + gi
                    acc = ACC[(base[0] + g) % 2]
                    take(base[0] + gi)
                    dve.wait_ge(sem("up_centre"), n * 4 + 2 * tiles)
                    order = [(t, t if tiles == 2 else 2 * t) for t in range(2 * tiles)]
                    for t, i in order:
                        w = gi * 16 + (VEC["ffn_conv"][0] + 16 * base[1] + 4 * i)
                        ins = V.scalar_tensor_tensor(out=Y[:, i, 1:T], in0=acc[:, t, 0:T - 1],
                                                     scalar=VV[:, bass.ds(w, 1)], in1=Y[:, i, 1:T],
                                                     op0=ALU.mult, op1=ALU.add)
                    ins.then_inc(sem("up_left"), 1)
                    dve.wait_ge(sem("up_left"), n + 1)
                    for t, i in order:
                        w = gi * 16 + (VEC["ffn_conv"][0] + 16 * base[1] + 4 * i)
                        ins = V.scalar_tensor_tensor(out=Y[:, i, 0:T - 1], in0=acc[:, t, 1:T],
                                                     scalar=VV[:, bass.ds(w + 2, 1)], in1=Y[:, i, 0:T - 1],
                                                     op0=ALU.mult, op1=ALU.add)
                    ins.then_inc(sem("up_conv"), 1)
                    V.engine_nop().then_inc(acc_free, 1)
                    dve.wait_ge(sem("up_silu"), n + 1)
                    V.tensor_tensor(Y[:, 6:6 + tiles, :], Y[:, 0:tiles, :], Y[:, 4:4 + tiles, :], ALU.mult)\
                        .then_inc(sem("up_prod"), 1)
                    dve.wait_ge(sem("up_hi"), n + 1)
                    V.tensor_tensor(UL[:, bass.ds(gi * 2, tiles), :], Y[:, 6:6 + tiles, :],
                                    UH[:, bass.ds(gi * 2, tiles), :].bitcast(F32), ALU.subtract)\
                        .then_inc(sem("up_done"), 1)
                return evac

            for n, (a, b) in enumerate(PARTS):
                ev = up_evac((PH[f"up{n}"][1], a // 2))
                full = (b - a) // 2
                phase(f"up{n}", full, evac=ev)
                if (b - a) % 2:
                    for j in range(2):
                        split(PH[f"up{n}"][0] + 4 * full + j)
                    flush()
                    pending[0] = lambda ev=ev, full=full: ev(full % 2, full // 2, tiles=1)
                res = residual(f"down{n}", 5 * KD)
                if n < 2:
                    phase(f"down{n}", 4, evac=res)
                else:
                    c0 = PH["down2"][0]
                    for j in range(12):
                        split(c0 + j)
                        if j == 1:
                            flush()
                        if j % 3 == 1 and j > 1:
                            g = j // 3 - 1
                            res(g % 2, g // 2)

            def angles():
                dve.wait_ge(sem("positions_loaded"), 16)
                link(V.tensor_copy(R2[:, 0:T], POS[:, :]))
                for i, inv in enumerate(("inv2", "invi")):
                    r, n, m = Y[:, i, :], R2[:, 2 * T:3 * T], R2[:, 3 * T:4 * T]
                    link(V.tensor_scalar(r, R2[:, 0:T], con(inv), None, ALU.mult))
                    link(V.tensor_scalar(n, r, 1.0 / (2 * np.pi), 12582912.0, ALU.mult, ALU.add))
                    link(V.tensor_scalar(n, n, -12582912.0, None, ALU.add))
                    for part in (6.28125, 1.9350051879882812e-03, 3.0199157663446332e-07):
                        link(V.scalar_tensor_tensor(out=r, in0=n, scalar=-part, in1=r, op0=ALU.mult, op1=ALU.add))
                    link(V.tensor_scalar(r, r, 3.141592, -3.141592, ALU.min, ALU.max))
                V.engine_nop().then_inc(sem("angles"), 1)

            def enter2():
                dve.wait_ge(acc_free, PH["ikw"][1])
                V.engine_nop().then_inc(sem("n2_in"), 1)
                total("n2", Y[:, :, :], T)
                variance("n2", T, D, EPS)
                normed("n2", X, X, lambda k: vec("g_final", k), None)
                lo_of(X, AH, AL, "n2_hi", done="a_ready")
                angles()
            c0, g0 = PH["ikw"]
            last = PH["down2"][1] + 3
            pending[0] = lambda: (residual("down2", 5 * KD)(1, 1), enter2())
            for j in range(2):
                split(c0 + j)
                if j == 1:
                    flush()

            def ikw_evac():
                take(g0)
                V.tensor_copy(Y[:, 12, :], ACC[g0 % 2][:, 0, :])
                V.tensor_copy(IW[:, :, :], ACC[g0 % 2][:, 2, 0:32].rearrange("p (a b) -> p a b", a=2))\
                    .then_inc(acc_free, 1)
                V.engine_nop().then_inc(sem("ik"), 1)
            pending[0] = ikw_evac
            phase("iq", 2, evac=copy_out("iq", Y, 4))
            flush()
            V.engine_nop().then_inc(sem("iq"), 1)
            dve.wait_ge(sem("tables"), 4)
            for b in range(3):
                n = 4 if b < 2 else 1
                dve.wait_ge(sem("index_rot"), b + 1)
                x = Y[:, 4 + 4 * b:4 + 4 * b + n, :]
                w = R1[:, 0:n * T].rearrange("p (a t) -> p a t", t=T)
                v = R2[:, 0:n * T].rearrange("p (a t) -> p a t", t=T)
                rot = AUX[:, 0:2, :].rearrange("p a (b t) -> p (a b) t", t=T)[:, 0:n, :] if b != 1 else \
                    AUX[:, 2:4, :].rearrange("p a (b t) -> p (a b) t", t=T)
                rope(x, rot, wide_bcast(COSI[:, :], n), wide_bcast(SINI[:, :], n), w, v)
                V.engine_nop().then_inc(sem("index_in"), 1)
            for u in range(IH):
                qt, h = u // 8, 2 * (u % 8)
                dve.wait_ge(sem("index_relu"), u + 1)
                for i in range(2):
                    acc = Y[:, 13 + qt, :] if i == 0 else R1[:, T * qt:T * qt + T]
                    x = R2[:, 512 * (u % 2) + T * i:512 * (u % 2) + T * i + T]
                    s = IW[:, qt, h + i:h + i + 1]
                    if h == 0:
                        V.tensor_scalar(acc, x, s, None, ALU.mult).then_inc(sem("index_added"), 1)
                    else:
                        dve.wait_ge(sem("index_added"), 2 * u + i - 1)
                        V.scalar_tensor_tensor(out=acc, in0=x, scalar=s, in1=acc, op0=ALU.mult, op1=ALU.add)\
                            .then_inc(sem("index_added"), 1)
                if h == 14:
                    dve.wait_ge(sem("index_added"), 2 * u + 2)
                    V.tensor_tensor(Y[:, 13 + qt, :], Y[:, 13 + qt, :], R1[:, T * qt:T * qt + T], ALU.add)\
                        .then_inc(sem("index_scored"), 1)
            for qt in range(2):
                dve.wait_ge(sem("index_masked"), qt + 1)
                work = Y[:, 13 + qt, :]
                for r in range(TOPK // 8):
                    link(V.max(COL[:, 48:56], work))
                    link(V.match_replace(out=work, in_to_replace=COL[:, 48:56], in_values=work, imm_value=MARK))
                V.tensor_scalar(BIASM[:, qt, :], work, MARK, BIG, ALU.is_equal, ALU.mult).then_inc(sem("chosen"), 1)
            for qt in range(2):
                dve.wait_ge(sem("chosen_masked"), qt + 1)
                link(V.tensor_scalar(BIASM[:, qt, :], BIASM[:, qt, :], -BIG, None, ALU.add))

            def token_major(name, dst):
                g0 = PH[name][1]

                def evac(g, reg):
                    take(g0)
                    V.tensor_copy(dst, ACC[g0 % 2][:, :, :].rearrange("p a b -> p (a b)")).then_inc(acc_free, 1)
                return evac

            phase("k_a", 1, evac=copy_out("k_a", Y, 0))
            phase("v_a", 1, evac=token_major("v_a", R0[:, :]))
            phase("q_a", 4, evac=copy_out("q_a", U, 0))

            def gate_then(tag):
                def f():
                    dve.wait_ge(acc_free, PH["att2" if tag == "a" else "att3"][1])
                    V.engine_nop().then_inc(sem("gate_" + tag), 1)
                return f
            phase("gate_a", 4, evac=copy_out("gate_a", U, KD), then=gate_then("a"))
            flush()
            for b in range(5):
                x = Y[:, 0:4, :] if b == 0 else U[:, 4 * b - 4:4 * b, :]
                dve.wait_ge(sem("a_rot"), b + 1)
                a = 2 * (b % 2)
                rope(x, AUX[:, a:a + 2, :].rearrange("p a (b t) -> p (a b) t", t=T), wide_bcast(COS2[:, :], 4),
                     wide_bcast(SIN2[:, :], 4), R1[:, :].rearrange("p (a t) -> p a t", t=T),
                     R2[:, :].rearrange("p (a t) -> p a t", t=T))
                V.engine_nop().then_inc(sem("a_in"), 1)

            g0 = PH["att2"][1]

            def weighted2(h):
                dve.wait_ge(sem("exp2"), h + 1)
                link(V.reciprocal(COL[:, 16 + 2 * (h % 2):18 + 2 * (h % 2)],
                                  COL[:, 4 * (h % 2) + 2:4 * (h % 2) + 4]))
                for qt in range(2):
                    s = PB[h % 2][:, T * qt:T * qt + T]
                    k = 16 + 2 * (h % 2) + qt
                    ins = V.tensor_scalar(s, s, COL[:, k:k + 1], None, ALU.mult)
                ins.then_inc(sem("normed2"), 1)

            def gated(h, g0, tag):
                if h == 0:
                    dve.wait_ge(sem("silu_" + tag), 1)
                take(g0 + h)
                V.tensor_tensor(U[:, h, :], ACC[(g0 + h) % 2][:, 0, :], U[:, KD + h, :], ALU.mult)\
                    .then_inc(acc_free, 1)

            for h in range(NH2):
                dve.wait_ge(sem("scores2"), h + 1)
                if h >= 2:
                    dve.wait_ge(sem("turned2"), h - 1)
                link(V.scalar_tensor_tensor(out=PB[h % 2][:, :], in0=AUX[:, h % 2, :], scalar=HD ** -0.5,
                                            in1=BIASM[:, :, :].rearrange("p a t -> p (a t)"),
                                            op0=ALU.mult, op1=ALU.add))
                k = 20 + 2 * (h % 2)
                link(V.tensor_reduce(COL[:, k:k + 2], PB[h % 2][:, :].rearrange("p (a t) -> p a t", a=2),
                                     AX.X, ALU.max))
                V.tensor_scalar(COL[:, 4 * (h % 2):4 * (h % 2) + 2], COL[:, k:k + 2], -1.0, None, ALU.mult)\
                    .then_inc(sem("max2"), 1)
                if h:
                    weighted2(h - 1)
                if h >= 2:
                    gated(h - 2, g0, "a")
            weighted2(NH2 - 1)
            gated(NH2 - 2, g0, "a")
            gated(NH2 - 1, g0, "a")

            def out_split(tag, nxt):
                def f():
                    dve.wait_ge(acc_free, PH[nxt][1])
                    V.engine_nop().then_inc(sem("att_" + tag), 1)
                    lo_of(U, AH, AL, "att_hi_" + tag, done="att_ready_" + tag)
                return f
            pending[0] = out_split("a", "o_a")

            def add_alpha(name):
                g0 = PH[name][1]

                def evac(g, reg):
                    gi = 2 * reg + g
                    take(g0 + gi)
                    x = X[:, bass.ds(gi * 4, 4), :]
                    V.scalar_tensor_tensor(out=x, in0=x, scalar=ALPHA, in1=ACC[(g0 + g) % 2][:, :, :],
                                           op0=ALU.mult, op1=ALU.add).then_inc(acc_free, 1)
                return evac

            def layer_norm(i):
                def f():
                    n = f"ln{i}"
                    dve.wait_ge(acc_free, PH[f"pgate{i}"][1])
                    link(V.tensor_reduce(RSTD[:, 0:T], X[:, :, :].rearrange("p k t -> p t k"), AX.X, ALU.add))
                    V.engine_nop().then_inc(sem(n + "_sum"), 1)
                    dve.wait_ge(sem(n + "_mean"), 1)
                    link(V.tensor_scalar(RSTD[:, T:2 * T], AUX[:, 1, 0:T], 1.0 / D, None, ALU.mult))
                    for q in range(4):
                        s = slice(4 * q, 4 * q + 4)
                        V.tensor_tensor(X[:, s, :], X[:, s, :], wide_bcast(RSTD[:, T:2 * T], 4), ALU.subtract)\
                            .then_inc(sem(n + "_centred"), 1)
                    total(n, Y[:, :, :], T)
                    variance(n, T, D, LN_EPS)
                    normed(n, X, X, lambda k: vec("ln_g", KD * i + k), lambda k: vec("ln_b", KD * i + k))
                    lo_of(X, AH, AL, n + "_hi", done=n + "_ready")
                return f

            phase("o_a", 4, evac=add_alpha("o_a"), then=layer_norm(0))
            dve.wait_ge(sem("p_hi"), 1)
            V.tensor_tensor(PTL[:, :, :], PRAW[:, :, :], PTH[:, :, :].bitcast(F32),
                            ALU.subtract).then_inc(sem("p_ready"), 1)

            def embed(i, then):
                def gate_out():
                    dve.wait_ge(acc_free, PH[f"ple{i}"][1])
                    V.engine_nop().then_inc(sem(f"pgate{i}_out"), 1)
                phase(f"pgate{i}", 4, evac=copy_out(f"pgate{i}", U, 0), then=gate_out)
                c0, g0 = PH[f"ple{i}"]
                split(c0)
                split(c0 + 1)
                flush()

                def ple():
                    dve.wait_ge(sem(f"pgate{i}_sig"), 1)
                    for g in range(4):
                        take(g0 + g)
                        s = slice(4 * g, 4 * g + 4)
                        V.tensor_tensor(U[:, s, :], U[:, s, :], ACC[(g0 + g) % 2][:, :, :], ALU.mult)\
                            .then_inc(acc_free, 1)
                    for g in range(4):
                        dve.wait_ge(acc_free, g0 + g + 1)
                        s = slice(4 * g, 4 * g + 4)
                        V.tensor_tensor(X[:, s, :], X[:, s, :], U[:, s, :], ALU.add)\
                            .then_inc(sem("x1_full" if i == 0 else "x2_full"), 1)
                ple()
                pending[0] = then

            embed(0, lambda: lo_of(X, AH, AL, "x1_hi", done="b_ready"))
            phase("k_b", 1, evac=copy_out("k_b", Y, 0))
            phase("v_b", 1, evac=token_major("v_b", R0[:, :]))
            phase("q_bb", 4, evac=copy_out("q_bb", U, 0))
            phase("gate_b", 4, evac=copy_out("gate_b", U, KD), then=gate_then("b"))
            flush()
            g0 = PH["att3"][1]
            strict = con("strict")

            def softplus(h):
                dve.wait_ge(sem("act3"), 4 * h + 3)
                V.scalar_tensor_tensor(out=PB[h % 2][:, :], in0=ZS[h % 2], scalar=0.0, in1=PB[h % 2][:, :],
                                       op0=ALU.max, op1=ALU.add).then_inc(sem("sp3"), 1)

            def log_weight(h):
                dve.wait_ge(sem("suffix3"), h + 1)
                V.tensor_tensor(ZS[h % 2], ZS[h % 2], AUX[:, 2 + h % 2, :], ALU.add).then_inc(sem("w3"), 1)

            for h in range(NH2):
                dve.wait_ge(sem("scores3"), h + 1)
                z = ZS[h % 2]
                if h >= 2:
                    dve.wait_ge(sem("act3"), 4 * (h - 1))
                V.scalar_tensor_tensor(out=z[:, 0:P], in0=AUX[:, h % 2, 0:P], scalar=HD ** -0.5, in1=strict,
                                       op0=ALU.mult, op1=ALU.add)
                V.tensor_scalar(z[:, P:T], AUX[:, h % 2, P:T], HD ** -0.5, None, ALU.mult)
                V.tensor_scalar(z[:, T:T + P], AUX[:, h % 2, T:T + P], HD ** -0.5, -BIG, ALU.mult, ALU.add)
                V.scalar_tensor_tensor(out=z[:, T + P:2 * T], in0=AUX[:, h % 2, T + P:2 * T], scalar=HD ** -0.5,
                                       in1=strict, op0=ALU.mult, op1=ALU.add).then_inc(sem("z3"), 1)
                softplus(h)
                if h:
                    gated(h - 1, g0, "b")
                log_weight(h)
            gated(NH2 - 1, g0, "b")
            pending[0] = out_split("b", "o_b")
            phase("o_b", 4, evac=add_alpha("o_b"), then=layer_norm(1))
            embed(1, lambda: None)
            flush()
            dve.wait_ge(sem("x2_full"), 4)
            V.engine_nop().then_inc(sem("result"), 1)

        @block.tensor
        def _(pe):
            TE = nc.tensor

            def mm(out, lhs, rhs, start, stop):
                return TE.matmul(out, lhs, rhs, start=start, stop=stop, skip_group_check=True)

            def three(out, w_hi, w_lo, x_hi, x_lo, start, stop, weights_move=False):
                if weights_move:
                    mm(out, x_hi, w_hi, start, False)
                    mm(out, x_hi, w_lo, False, False)
                    return mm(out, x_lo, w_hi, False, stop)
                mm(out, w_hi, x_hi, start, False)
                mm(out, w_hi, x_lo, False, False)
                return mm(out, w_lo, x_hi, False, stop)

            def chunk_ready(c, reg=None, step=0):
                pe.wait_ge(lo_done, c + 1 if reg is None else reg * step + (c + 1))

            def acc_ready(g, reg=None, step=0):
                if g >= 2:
                    pe.wait_ge(acc_free, g - 1 if reg is None else reg * step + (g - 1))

            def group(c, g, xh, xl, reg=None, tiles=4, ks=(4, 4, 4, 4), width=512, weights_move=False,
                      extra=None):
                acc_ready(g, reg, 2)
                acc = ACC[g % 2]
                k0, K = 0, sum(ks)
                for j, nk in enumerate(ks):
                    cc = c + j
                    chunk_ready(cc, reg, 8)
                    hi = HI[cc % 2][:, 0:nk * width].rearrange("p (k n) -> p k n", n=width)
                    lo = LO[cc % 2][:, 0:nk * width].rearrange("p (k n) -> p k n", n=width)
                    for k in range(nk):
                        kk = k0 + k
                        first, last = kk == 0, kk == K - 1
                        if weights_move:
                            for t in range(2):
                                s = slice(P * t, P * t + P)
                                ins = three(acc[:, 2 * t:2 * t + 2, :].rearrange("p a b -> p (a b)"),
                                            hi[:, k, :], lo[:, k, :], xh[:, kk, s], xl[:, kk, s],
                                            first, last, weights_move=True)
                            continue
                        for t in range(tiles):
                            s = slice(P * t, P * t + P)
                            ins = three(acc[:, t, :], hi[:, k, s], lo[:, k, s], xh[:, kk, :], xl[:, kk, :],
                                        first and t % 2 == 0, last)
                        if extra:
                            ins = extra(hi, lo, k, kk, first, last)
                    ins.then_inc(pe_chunk, 1)
                    k0 += nk
                pe.wait_ge(pe_chunk, c + len(ks) if reg is None else reg * 8 + (c + len(ks)))
                pe.sem_inc(acc_full, 1)

            def ada_reduce(bufs, fmas, outs):
                pe.wait_ge(ada_fma, fmas)
                if outs is not None:
                    pe.wait_ge(ada_out, outs)
                for v, b in enumerate(bufs):
                    for t in range(4):
                        for i in range(2):
                            ins = mm(AUX[:, 3, 8 * v + t:8 * v + t + 1], b[:, i, P * t:P * t + P], ONES[:, 0:1],
                                     i == 0, i == 1)
                ins.then_inc(ada_sum, 1)

            def carry(name, g, reg=None):
                if name not in CARRY:
                    return
                first, per = CARRY[name]
                if per == 2:
                    if g == 0:
                        return
                    ag = first + (0 if reg is None else reg)
                    buf = FMA[0]
                else:
                    ag = first + g + (0 if reg is None else 2 * reg)
                    buf = FMA[(first + g) % 2]
                ada_reduce([buf], (ag - GTL) * 16 + (C0_FMAS + 16), ag + GTL)

            def phase(name, n, ready=None, xh=AH, xl=AL, **kw):
                c0, g0 = PH[name]
                if ready:
                    pe.wait_ge(*since(ready, 1))
                if n == 1:
                    group(c0, g0, xh, xl, **kw)
                    carry(name, 0)
                    return
                with pe.Fori(0, n // 2) as i:
                    for g in range(2):
                        group(c0 + 4 * g, g0 + g, xh, xl, reg=i, **kw)
                        carry(name, g, i)
                if n % 2:
                    group(c0 + 4 * (n - 1), g0 + n - 1, xh, xl, **kw)

            def totals(name, w, bank=0, ready="_ss", done="_tot"):
                pe.wait_ge(*since(name + ready, 1))
                mm(AUX[:, bank, 0:w], ONES[:, :], RSTD[:, 0:w], True, True).then_inc(step(name + done)[0], 1)

            pe.wait_ge(sem("ones"), 1)
            totals("nx", T)
            pe.wait_ge(*since("nx_std", 1))
            totals("nc", T)
            for ag in range(GTL):
                ada_reduce([FMA[ag % 2], FMA[2 + ag % 2]], 32 * (ag + 1), 2 * ag if ag else None)

            pe.wait_ge(sem("in_ready"), 1)
            pe.wait_ge(sem("ctx_ready"), 1)

            def context(hi, lo, k, kk, first, last):
                for t in range(3):
                    s = slice(P * t, P * t + P)
                    o = AUX[:, t // 2, T * (t % 2):T * (t % 2) + T]
                    ins = three(o, hi[:, k, s], lo[:, k, s], UH[:, kk, :], UL[:, kk, :], first and t % 2 == 0, last)
                return ins
            phase("kv_in", 1, tiles=3, width=384, extra=context)
            phase("q_in", 1)
            totals("nkv", 512)
            pe.wait_ge(*since("nkv_std", 1))
            totals("nq", T)
            pe.wait_ge(sem("consts_loaded"), 16)
            pe.wait_ge(sem("kr_copied"), 1)
            mm(AUX[:, 1, 0:T], con("rot1"), KR[:, 0:T], True, True).then_inc(sem("kr_rot"), 1)
            phase("conv_in", 6)
            c0, g0 = PH["q_b"]
            pe.wait_ge(sem("q_ready"), 1)
            for i in range(4):
                group(c0 + i, g0 + i, QH, QL, tiles=3, ks=(4,), width=384)
            c0, g0 = PH["kv_b"]
            pe.wait_ge(sem("kv_ready"), 1)
            for half in range(2):
                c = c0 + half
                chunk_ready(c)
                hi = HI[c % 2][:, :].rearrange("p (k n) -> p k n", k=2)
                lo = LO[c % 2][:, :].rearrange("p (k n) -> p k n", k=2)
                for i in range(4):
                    g = g0 + 4 * half + i
                    acc_ready(g)
                    a = ACC[g % 2][:, :, :].rearrange("p a b -> p (a b)")
                    for k in range(2):
                        for t in range(2):
                            o = a[:, 512 * t:512 * t + 512]
                            if half == 0:
                                s = slice(P * (2 * i + t), P * (2 * i + t) + P)
                                ins = three(o, hi[:, k, s], lo[:, k, s], KVH[:, k, :], KVL[:, k, :], k == 0, k == 1)
                            else:
                                s = slice(512 * t, 512 * t + 512)
                                q = slice(P * i, P * i + P)
                                ins = three(o, hi[:, k, s], lo[:, k, s], KVH[:, k, q], KVL[:, k, q], k == 0, k == 1,
                                            weights_move=True)
                    if i < 3:
                        ins.then_inc(acc_full, 1)
                    else:
                        ins.then_inc(pe_chunk, 1)
                        pe.wait_ge(pe_chunk, c + 1)
                        pe.sem_inc(acc_full, 1)
            pe.wait_ge(sem("qt1"), 1)
            for i in range(4):
                ins = mm(AUX[:, i // 2, T * (i % 2):T * (i % 2) + T], con("rot1"), QT1[:, 8 + i, :],
                         i % 2 == 0, i % 2 == 1)
            ins.then_inc(sem("q_rot"), 1)

            pe.wait_ge(sem("att1_in"), 1)
            g0 = PH["att1"][1]

            def scores(u):
                h, qt = u // 2, u % 2
                q = slice(P * qt, P * qt + P)
                r = slice(ROPE * (h % 2), ROPE * (h % 2) + ROPE)
                if u >= 2:
                    pe.wait_ge(sem("exp1"), u - 1)
                mm(AUX[:, u % 2, :], QT1[:, h, q], KN1[:, h, :], True, False)
                mm(AUX[:, u % 2, :], QT1[r, 8 + h // 2, q], KR[r, :], False, True).then_inc(sem("scores1"), 1)

            def turn(u):
                pe.wait_ge(sem("normed1"), u + 1)
                if u >= 2:
                    pe.wait_ge(sem("probs1"), u - 1)
                for k in range(4):
                    ins = TE.transpose(AUX[:, 2 + u % 2, P * k:P * k + P], PB[u % 2][:, P * k:P * k + P], IDENT)
                ins.then_inc(sem("turned1"), 1)

            def values(h):
                acc_ready(g0 + h)
                pe.wait_ge(sem("probs1"), 2 * h + 2)
                for k in range(4):
                    ins = mm(ACC[(g0 + h) % 2][:, 0, :], V1[:, k, P * h:P * h + P], PT[h % 2][:, k, :],
                             k == 0, k == 3)
                ins.then_inc(acc_full, 1)

            scores(0)
            for u in range(2 * NH1):
                if u + 1 < 2 * NH1:
                    scores(u + 1)
                turn(u)
                if u % 2 == 0 and u:
                    values(u // 2 - 1)
            values(NH1 - 1)
            for b in range(4):
                pe.wait_ge(sem("mix_sq"), b + 1)
                if b >= 2:
                    pe.wait_ge(sem("mix_var"), b - 1)
                for i in range(2):
                    ins = mm(AUX[:, 2 * (b % 2) + i, :], ONES[:, :],
                             U[:, 8 + 2 * i:10 + 2 * i, :].rearrange("p a b -> p (a b)"), True, True)
                ins.then_inc(sem("mix_tot"), 1)
            pe.wait_ge(sem("mix_var"), 4)
            phase("w_out", 4, ready="mix_ready")
            totals("nf", T)
            pe.wait_ge(sem("ffn_ready"), 1)
            for n, (a, b) in enumerate(PARTS):
                phase(f"up{n}", (b - a) // 2)
                if (b - a) % 2:
                    full = (b - a) // 2
                    c0, g0 = PH[f"up{n}"]
                    group(c0 + 4 * full, g0 + full, AH, AL, tiles=2, ks=(8, 8), width=256)
                pe.wait_ge(sem("up_done"), (b + 1) // 2)
                if n < 2:
                    phase(f"down{n}", 4, xh=UH, xl=UL)
                else:
                    c0, g0 = PH[f"down{n}"]
                    for g in range(4):
                        group(c0 + 3 * g, g0 + g, UH, UL, ks=(4, 4, 3))
            totals("n2", T)
            pe.wait_ge(sem("consts2_loaded"), 16)
            pe.wait_ge(sem("minus_ones"), 1)
            pe.wait_ge(sem("a_ready"), 1)
            c0, g0 = PH["ikw"]
            acc_ready(g0)
            for j in range(2):
                c = c0 + j
                chunk_ready(c)
                hi = HI[c % 2][:, 0:8 * 144].rearrange("p (k n) -> p k n", n=144)
                lo = LO[c % 2][:, 0:8 * 144].rearrange("p (k n) -> p k n", n=144)
                for k in range(8):
                    kk = 8 * j + k
                    three(ACC[g0 % 2][:, 0, :], hi[:, k, 0:P], lo[:, k, 0:P], AH[:, kk, :], AL[:, kk, :],
                          kk == 0, kk == KD - 1)
                    for t in range(2):
                        s = slice(P * t, P * t + P)
                        ins = three(ACC[g0 % 2][:, 2, IH * t:IH * t + IH], hi[:, k, P:P + IH], lo[:, k, P:P + IH],
                                    AH[:, kk, s], AL[:, kk, s], kk == 0 and t == 0, kk == KD - 1, weights_move=True)
                ins.then_inc(pe_chunk, 1)
            pe.wait_ge(pe_chunk, c0 + 2)
            pe.sem_inc(acc_full, 1)
            phase("iq", 2)
            pe.wait_ge(sem("iq"), 1)
            pe.wait_ge(sem("ik"), 1)
            for b in range(3):
                if b == 2:
                    pe.wait_ge(sem("index_in"), 1)
                for t in range(4 if b < 2 else 1):
                    a = 2 * (b % 2) + t // 2
                    ins = mm(AUX[:, a, T * (t % 2):T * (t % 2) + T], con("roti"), Y[:, 4 + 4 * b + t, :],
                             t % 2 == 0, True)
                ins.then_inc(sem("index_rot"), 1)
            pe.wait_ge(sem("index_in"), 3)
            for u in range(IH):
                qt, pair = u // 8, u % 8
                if u >= 2:
                    pe.wait_ge(sem("index_relu"), u - 1)
                for i in range(2):
                    r = slice(ID * i, ID * i + ID)
                    ins = mm(AUX[:, 2 * (u % 2) + i, 0:T], Y[r, 4 + pair, P * qt:P * qt + P], Y[r, 12, :],
                             True, True)
                ins.then_inc(sem("index_dots"), 1)
            phase("k_a", 1)
            phase("v_a", 1, weights_move=True)
            phase("q_a", 4)
            phase("gate_a", 4)
            pe.wait_ge(sem("gate_a"), 1)
            pe.wait_ge(sem("index_relu"), IH)
            for b in range(5):
                if b >= 2:
                    pe.wait_ge(sem("a_in"), b - 1)
                for t in range(4):
                    x = Y[:, t, :] if b == 0 else U[:, 4 * b - 4 + t, :]
                    ins = mm(AUX[:, 2 * (b % 2) + t // 2, T * (t % 2):T * (t % 2) + T], con("rot2"), x,
                             t % 2 == 0, True)
                ins.then_inc(sem("a_rot"), 1)
            pe.wait_ge(sem("a_in"), 5)
            g0 = PH["att2"][1]

            def scores2(h):
                if h >= 2:
                    pe.wait_ge(sem("max2"), h - 1)
                for qt in range(2):
                    ins = mm(AUX[:, h % 2, T * qt:T * qt + T], U[:, h, P * qt:P * qt + P], Y[:, h // 4, :],
                             qt == 0, True)
                ins.then_inc(sem("scores2"), 1)

            def turn2(h):
                pe.wait_ge(sem("normed2"), h + 1)
                if h >= 2:
                    pe.wait_ge(sem("probs2"), h - 1)
                for kt in range(2):
                    for qt in range(2):
                        ins = TE.transpose(AUX[:, 2 + h % 2, T * kt + P * qt:T * kt + P * qt + P],
                                           PB[h % 2][:, T * qt + P * kt:T * qt + P * kt + P], IDENT)
                ins.then_inc(sem("turned2"), 1)

            def values2(h, w, ready, count):
                acc_ready(g0 + h)
                pe.wait_ge(*since(ready, count))
                for kt in range(2):
                    ins = mm(ACC[(g0 + h) % 2][:, 0, :], R0[:, 512 * kt + P * (h // 4):512 * kt + P * (h // 4) + P],
                             w(kt), kt == 0, kt == 1)
                ins.then_inc(acc_full, 1)

            scores2(0)
            for h in range(NH2):
                if h + 1 < NH2:
                    scores2(h + 1)
                turn2(h)
                if h:
                    values2(h - 1, lambda kt: PT2[(h - 1) % 2][:, kt, :], "probs2", h)
            values2(NH2 - 1, lambda kt: PT2[(NH2 - 1) % 2][:, kt, :], "probs2", NH2)
            phase("o_a", 4, ready="att_ready_a")

            def norm_sums(i):
                totals(f"ln{i}", T, bank=1, ready="_sum", done="_mean")
                totals(f"ln{i}", T)
                pe.wait_ge(sem(f"ln{i}_ready"), 1)

            def embed(i):
                norm_sums(i)
                phase(f"pgate{i}", 4)
                c0, g0 = PH[f"ple{i}"]
                if i == 0:
                    pe.wait_ge(sem("p_ready"), 1)
                for j in range(2):
                    c = c0 + j
                    chunk_ready(c)
                    hi = HI[c % 2][:, :].rearrange("p (k n) -> p k n", k=2)
                    lo = LO[c % 2][:, :].rearrange("p (k n) -> p k n", k=2)
                    for half in range(2):
                        g = g0 + 2 * j + half
                        acc_ready(g)
                        for k in range(2):
                            for t in range(4):
                                s = slice(512 * half + P * t, 512 * half + P * t + P)
                                ins = three(ACC[g % 2][:, t, :], hi[:, k, s], lo[:, k, s], PTH[:, 2 * i + k, :],
                                            PTL[:, 2 * i + k, :], k == 0 and t % 2 == 0, k == 1)
                        if half == 0:
                            ins.then_inc(acc_full, 1)
                        else:
                            ins.then_inc(pe_chunk, 1)
                            pe.wait_ge(pe_chunk, c + 1)
                            pe.sem_inc(acc_full, 1)
            embed(0)
            pe.wait_ge(sem("b_ready"), 1)
            phase("k_b", 1)
            phase("v_b", 1, weights_move=True)
            phase("q_bb", 4)
            phase("gate_b", 4)
            pe.wait_ge(sem("gate_b"), 1)
            g0 = PH["att3"][1]

            def scores3(h):
                if h >= 2:
                    pe.wait_ge(sem("z3"), h - 1)
                for st in range(2):
                    ins = mm(AUX[:, h % 2, T * st:T * st + T], Y[:, h // 4, P * st:P * st + P], U[:, h, :],
                             st == 0, True)
                ins.then_inc(sem("scores3"), 1)

            def suffix3(h):
                pe.wait_ge(sem("sp3"), h + 1)
                a, sp = AUX[:, 2 + h % 2, :], PB[h % 2]
                mm(a[:, 0:T], con("tri"), sp[:, 0:T], True, False)
                mm(a[:, 0:T], MINUS[:, :], sp[:, T:2 * T], False, True)
                mm(a[:, T:2 * T], con("tri"), sp[:, T:2 * T], False, True).then_inc(sem("suffix3"), 1)

            scores3(0)
            for h in range(NH2):
                if h + 1 < NH2:
                    scores3(h + 1)
                suffix3(h)
                values2(h, lambda kt: PB[h % 2][:, T * kt:T * kt + T], "act3", 4 * h + 4)
            phase("o_b", 4, ready="att_ready_b")
            embed(1)


def _constants():
    out = np.zeros((P, NCON), np.float32)

    def put(name, a):
        at, n = CON[name]
        out[:, at:at + n] = a

    put("ident", np.eye(P))
    rot1 = np.zeros((P, P))
    for i in range(0, P, 2):
        rot1[i + 1, i] = -1.0
        rot1[i, i + 1] = 1.0
    put("rot1", rot1)
    rot2 = np.zeros((P, P))
    half = HD // 8
    for i in range(half):
        rot2[half + i, i] = -1.0
        rot2[i, half + i] = 1.0
    put("rot2", rot2)
    roti = np.zeros((P, P))
    ih = ID // 8
    for b in (0, ID):
        for i in range(ih):
            roti[b + ih + i, b + i] = -1.0
            roti[b + i, b + ih + i] = 1.0
    put("roti", roti)
    f = np.float32
    axis = ROPE // 2
    inv = f(10000.0) ** (-np.arange(0, axis, 2, dtype=f) / f(axis))
    t = np.arange(T)
    ang = np.concatenate([(t // 64).astype(f)[:, None] * inv, (t % 64).astype(f)[:, None] * inv], axis=-1)
    ang = ang.astype(f).astype(np.float64)
    lane = (np.arange(P) % ROPE) // 2
    put("cos1", np.cos(ang).T[lane])
    put("sin1", np.sin(ang).T[lane])
    put("tri", -(np.arange(P)[:, None] >= np.arange(P)[None, :]).astype(f))
    put("strict", np.where(np.arange(P)[:, None] < np.arange(P)[None, :], 0.0, -BIG))

    def freq(n):
        return (f(1.0) / (f(THETA) ** (np.arange(n, dtype=f) / f(n)))).astype(f)
    a = np.zeros((P, 1), f)
    a[0:half, 0] = a[half:2 * half, 0] = freq(half)
    put("inv2", a)
    a = np.zeros((P, 1), f)
    for b in (0, ID):
        a[b:b + ih, 0] = a[b + ih:b + 2 * ih, 0] = freq(ih)
    put("invi", a)
    put("half_pi", np.pi / 2)
    return out


def kernel(**inputs):
    import concourse.bacc as bacc
    from concourse import mybir
    from concourse.bass_utils import run_bass_kernel_spmd

    arr = {k: np.asarray(v) for k, v in inputs.items()}
    F32 = np.float32

    chunks, _ = schedule()
    stream = np.zeros((len(chunks), P, CHUNK), F32)
    for c, spec in enumerate(chunks):
        if spec is None:
            continue
        key, layer, ks, cols = spec
        w = arr[key]
        w = w[layer] if w.ndim == 3 else w
        rows = w[ks[0] * P:(ks[-1] + 1) * P].reshape(len(ks), P, -1)
        part = np.concatenate([rows[:, :, a:b] for a, b in cols], axis=2).transpose(1, 0, 2).reshape(P, -1)
        stream[c, :, :part.shape[1]] = part
    ada = arr["w_ada"][0].reshape(4, 4, P, 24, 512).transpose(3, 0, 2, 1, 4).reshape(96, P, CHUNK)

    def col(a):
        return a.reshape(-1, P).T

    vecs = np.zeros((P, NVEC), F32)

    def put(name, a):
        at, n = VEC[name]
        vecs[:, at:at + n] = a

    put("c", col(arr["c"][0]))
    put("c_ctx", col(arr["c_ctx"]))
    put("b_ada", col(arr["b_ada"][0]))
    for name in ("g_mix_norm", "g_q_a", "g_kv_a", "g_mix_out", "g_ffn_norm"):
        put(name, col(arr[name][0]))
    put("g_final", col(arr["g_final"]))
    put("ln_g", col(arr["ln_g_2"].reshape(-1)))
    put("ln_b", col(arr["ln_b_2"].reshape(-1)))
    taps = np.stack([col(arr["conv_w"][0, i]) for i in range(3)] + [col(arr["conv_b"][0])], axis=2)
    put("conv", taps.reshape(P, -1))
    taps = np.stack([col(arr["ffn_conv_w"][0, i]) for i in range(3)] + [col(arr["ffn_conv_b"][0])], axis=2)
    a, g = taps[:, :FT], taps[:, FT:]
    order = []
    for f in range(0, FT, 2):
        n = min(2, FT - f)
        if n == 2:
            order += [a[:, f], a[:, f + 1], g[:, f], g[:, f + 1]]
        else:
            order += [a[:, f], np.zeros((P, 4), F32), g[:, f], np.zeros((P, 4), F32)]
    order = np.concatenate(order, axis=1)
    put("ffn_conv", np.pad(order, ((0, 0), (0, 0)))[:, :VEC["ffn_conv"][1]])

    def tokens(a):
        return np.ascontiguousarray(a.reshape(T, -1, P).transpose(2, 1, 0))

    p = arr["p_2"]
    data = {
        "stream": stream,
        "ada_stream": np.ascontiguousarray(ada),
        "vecs": vecs,
        "consts": _constants(),
        "x_t": tokens(arr["x"][0]),
        "ctx_t": tokens(arr["ctx"][0]),
        "p_t": np.concatenate([tokens(p[0, 0]), tokens(p[1, 0])], axis=1).reshape(P, 4 * T),
        "positions": np.broadcast_to(arr["positions_2"].reshape(1, T), (P, T)).copy(),
    }
    nc = bacc.Bacc("TRN2", target_bir_lowering=False, num_devices=1)
    args = [nc.dram_tensor(n, a.shape, mybir.dt.from_np(a.dtype), kind="ExternalInput").ap()
            for n, a in data.items()]
    out = nc.dram_tensor("out", (P, KD, T), mybir.dt.float32, kind="ExternalOutput").ap()
    two_blocks(nc, *args, out)
    r = run_bass_kernel_spmd(nc, [data], core_ids=[0])
    return r.results[0]["out"].transpose(2, 1, 0).reshape(1, T, D)
```

```python
import numpy as np

P = 128
T = 256
D = 2048
KD = D // P
CHUNK = 2048

NH1, NOPE, ROPE, VD = 8, 128, 64, 128
Q_RANK, KV_RANK, CONV_W = 512, 256, 1024
FFN = 5504
FT = FFN // P
PARTS = ((0, 16), (16, 32), (32, FT))
EPS, LN_EPS = 1e-6, 1e-5
NH2, NKV, HD = 16, 4, 128
IH, ID = 16, 64
TOPK = 64
THETA = 500000.0
ALPHA = 4.0 ** 0.25
NEG, MARK, BIG = -3.0e38, -3.4e38, 1.0e30

VEC = {}
_at = 0
for _name, _n in (("c", KD), ("c_ctx", KD), ("b_ada", 6 * KD), ("g_mix_norm", KD), ("g_q_a", 4), ("g_kv_a", 2),
                  ("conv", 8 * 4), ("g_mix_out", KD), ("g_ffn_norm", KD), ("ffn_conv", (FT + 1) // 2 * 16), ("g_final", KD),
                  ("ln_g", 2 * KD), ("ln_b", 2 * KD)):
    VEC[_name] = (_at, _n)
    _at += _n
NVEC = _at
CON = {}
_at = 0
for _name, _n in (("ident", P), ("rot1", P), ("cos1", T), ("sin1", T), ("inv2", 1), ("invi", 1), ("half_pi", 1),
                  ("rot2", P), ("roti", P), ("tri", P), ("strict", P)):
    CON[_name] = (_at, _n)
    _at += _n
NCON = _at
NCON1 = CON["rot2"][0]


def schedule():
    chunks, phases = [], {}
    groups = [0]

    def phase(name):
        phases[name] = (len(chunks), groups[0])

    def group(key, cols, ks=range(KD), per=4, layer=0, n_groups=1):
        ks = list(ks)
        for j in range(0, len(ks), per):
            chunks.append((key, layer, ks[j:j + per], cols))
        groups[0] += n_groups

    def wide(name, key, first, n, layer=0):
        phase(name)
        for g in range(n):
            group(key, [(first + 512 * g, first + 512 * (g + 1))], layer=layer)

    kr = (Q_RANK + KV_RANK, Q_RANK + KV_RANK + ROPE)
    phase("kv_in")
    group("w_in", [(Q_RANK, Q_RANK + KV_RANK), kr, kr])
    phase("q_in")
    group("w_in", [(0, Q_RANK)])
    wide("conv_in", "w_in", kr[1], 6)
    phase("q_b")
    hw = NOPE + ROPE
    for h in range(0, NH1, 2):
        nope = [(hw * i, hw * i + NOPE) for i in (h, h + 1)]
        rope = [(hw * i + NOPE, hw * (i + 1)) for i in (h, h + 1)]
        group("w_q_b", nope + rope, range(4))
    phase("kv_b")
    group("w_kv_b", [(256 * h, 256 * h + NOPE) for h in range(NH1)], range(2), n_groups=4)
    group("w_kv_b", [(256 * h + NOPE, 256 * (h + 1)) for h in range(NH1)], range(2), n_groups=4)
    phase("att1")
    groups[0] += NH1
    wide("w_out", "w_out", 0, 4)
    for n, (a, b) in enumerate(PARTS):
        phase(f"up{n}")
        for f in range(a, b, 2):
            w = P * min(2, b - f)
            group("w_up", [(P * f, P * f + w), (FFN + P * f, FFN + P * f + w)], per=CHUNK // (2 * w))
        phase(f"down{n}")
        for g in range(4):
            group("w_down", [(512 * g, 512 * (g + 1))], range(a, b))
    phase("ikw")
    group("w_in_a_2", [(6144, 6208), (6144, 6208), (6208, 6224)], per=8)
    wide("iq", "w_in_a_2", 5120, 2)
    phase("index")
    wide("k_a", "w_in_a_2", 2048, 1)
    wide("v_a", "w_in_a_2", 2560, 1)
    wide("q_a", "w_in_a_2", 0, 4)
    wide("gate_a", "w_in_a_2", 3072, 4)
    phase("att2")
    groups[0] += NH2
    wide("o_a", "w_o_a_2", 0, 4)

    def embed(i):
        wide(f"pgate{i}", "w_ple_gate_2", 0, 4, layer=i)
        phase(f"ple{i}")
        for g in range(2):
            group("w_ple_2", [(1024 * g, 1024 * (g + 1))], range(2), layer=i, n_groups=2)

    embed(0)
    wide("k_b", "w_kv_b_2", 0, 1)
    wide("v_b", "w_kv_b_2", 512, 1)
    wide("q_bb", "w_in_b_2", 0, 4)
    wide("gate_b", "w_in_b_2", D, 4)
    phase("att3")
    groups[0] += NH2
    wide("o_b", "w_o_b_2", 0, 4)
    embed(1)
    while len(chunks) % 4:
        chunks.append(None)
    return chunks, phases


def two_blocks(nc, stream, ada_stream, vecs, consts, x_t, ctx_t, p_t, positions, out):
    import concourse.bass as bass
    from concourse import mybir

    F32, F32R, I32 = mybir.dt.float32, mybir.dt.float32r, mybir.dt.int32
    ALU, ACT, AX = mybir.AluOpType, mybir.ActivationFunctionType, mybir.AxisListType
    chunks, PH = schedule()
    N_CHUNKS = len(chunks)
    WK = T * KD * 4

    at = [nc.sbuf_base + (-nc.sbuf_base) % 64]

    def place(name, shape, dt=F32, offset=None):
        size = int(np.prod(shape[1:])) * 4
        if offset is None:
            offset = at[0]
            at[0] += size + (-size) % 32
        return nc.alloc_sbuf_tensor_at(name, shape, dt, offset=offset)

    RAW = [place(f"raw{i}", [P, CHUNK]) for i in range(4)]
    HI = [place(f"hi{i}", [P, CHUNK], F32R) for i in range(2)]
    LO = [place(f"lo{i}", [P, CHUNK], F32R) for i in range(2)]
    X = place("x", [P, KD, T])
    o_ada = at[0]
    ADA = [place(f"ada_raw{i}", [P, CHUNK]) for i in range(2)]
    FMA = [place(f"ada_acc{i}", [P, 2, 512]) for i in range(2)]
    oA = at[0]; at[0] += WK
    oB = at[0]; at[0] += WK
    oY = at[0]; at[0] += WK
    oU = at[0]; at[0] += 2 * WK
    AH, AL = place("act_hi", [P, KD, T], F32R, oA), place("act_lo", [P, KD, T], F32R, oB)
    QT1 = place("q1", [P, 12, T], F32, oA)
    V1 = place("v1", [P, 4, 1024], F32, oB)
    SQC = place("ctx_squares", [P, KD, T], F32, oA)
    Y = place("y", [P, KD, T], F32, oY)
    KVH, KVL = place("kv_hi", [P, 2, 512], F32R, oY), place("kv_lo", [P, 2, 512], F32R, oY + 4096)
    QH, QL = place("qa_hi", [P, 4, T], F32R, oY + 8192), place("qa_lo", [P, 4, T], F32R, oY + 12288)
    U = place("u", [P, 2 * KD, T], F32, oU)
    UH, UL = place("u_hi", [P, KD, T], F32R, oU), place("u_lo", [P, KD, T], F32R, oU + WK)
    CTX = place("ctx", [P, KD, T], F32, oU + WK)
    ADA += [place(f"ada_raw{i}", [P, CHUNK], F32, oU + 4 * CHUNK * (i - 2)) for i in (2, 3)]
    KN1 = place("k_nope1", [P, NH1, 512], F32, oU + WK)
    R0 = place("r0", [P, 1024]); R1 = place("r1", [P, 1024]); R2 = place("r2", [P, 1024])
    KR = place("k_rope", [P, 512])
    CV = place("consts", [P, NCON1])
    VV = place("vectors", [P, NVEC])
    ONES = place("ones", [P, P])
    RSTD = place("rstd", [P, 512])
    SC = place("silu_c", [P, 2 * KD])
    MOD = place("ada", [P, 6 * KD])
    MODC = place("ada_ctx", [P, 2 * KD])
    SCL = place("scales", [P, 2 * KD])
    COL = place("columns", [P, 64])
    assert at[0] <= nc.sbuf_usable_end, (at[0], nc.sbuf_usable_end)
    o2 = [o_ada]

    def later(name, shape, dt=F32):
        t = place(name, shape, dt, o2[0])
        o2[0] += int(np.prod(shape[1:])) * 4
        return t

    PTH, PTL = later("p_hi", [P, 4, T], F32R), later("p_lo", [P, 4, T], F32R)
    COS2, SIN2, COSI, SINI = (later(n, [P, T]) for n in ("cos2", "sin2", "cosi", "sini"))
    BIASM = later("topk_bias", [P, 2, T])
    IW = later("index_weights", [P, 2, IH])
    PRAW = later("p_raw", [P, 4, T])
    ZS = [place(f"z{i}", [P, 512], F32, o2[0] - 4096 + 2048 * i)[:, :] for i in range(2)]
    MINUS = later("minus_ones", [P, P])
    CV2 = later("consts2", [P, NCON - NCON1])
    POS = later("positions", [P, T], I32)
    assert o2[0] <= oA
    PT2 = [R2[:, 512 * i:512 * i + 512].rearrange("p (k q) -> p k q", k=2) for i in range(2)]
    PB = [place(f"probs{i}", [P, 512], F32, oY + 8 * 1024 + 2048 * i) for i in range(4)]
    PT = [place(f"probs_t{i}", [P, 4, T], F32, oU + 8 * 1024 + 4096 * i) for i in range(2)]

    MIXV = [U[:, 8:12, :], U[:, 12:16, :], Y[:, 8:12, :], Y[:, 12:16, :]]

    def vec(name, i=0, n=1):
        a = VEC[name][0] + i
        return VV[:, a:a + n]

    def con(name):
        a, n = CON[name]
        return CV[:, a:a + n] if a < NCON1 else CV2[:, a - NCON1:a - NCON1 + n]

    IDENT = con("ident")
    ACC = [nc.alloc_psum_tensor(f"acc{i}", [P, 4, T], F32) for i in range(2)]
    AUX = nc.alloc_psum_tensor("aux", [P, 4, 512], F32)

    sems = {}

    def sem(name):
        if name not in sems:
            sems[name] = nc.alloc_semaphore(name)
        return sems[name]

    NORMS = {"nx": (2, 4), "nc": (2, 4), "nkv": (1, 1), "nq": (1, 1), "nf": (2, 4), "n2": (2, 4), "ln0": (2, 4),
             "ln1": (2, 4)}

    def step(name):
        norm, _, kind = name.rpartition("_")
        of = {"sq": 0, "full": 1, "hi": 1}
        if norm not in NORMS or kind not in ("sq", "ss", "tot", "var", "std", "full", "hi"):
            return sem(name), 0
        before = 0
        for other, counts in NORMS.items():
            if other == norm:
                break
            before += counts[of[kind]] if kind in of else 1
        return sem("norm_" + kind), before

    def since(name, n):
        s, before = step(name)
        return s, before + n

    raw_full = [sem(f"raw_full{i}") for i in range(4)]
    hi_done, lo_done, pe_chunk = sem("hi_done"), sem("lo_done"), sem("pe_chunk")
    acc_full, acc_free = sem("acc_full"), sem("acc_free")
    ada_full = [sem(f"ada_full{i}") for i in range(4)]
    ada_fma, ada_sum, ada_out = sem("ada_fma"), sem("ada_sum"), sem("ada_out")
    ada_used, ada_row, ada_row_out = sem("ada_used"), sem("ada_row"), sem("ada_row_out")
    GTL = 8
    TAKEN = 2 - GTL

    CARRY = {"kv_in": (8, 4), "q_in": (9, 4), "conv_in": (10, 4), "w_out": (16, 4), "up0": (20, 2)}

    with nc.Block() as block:

        @block.sync
        def _(eng):
            eng.dma_start(VV[:, :], vecs).then_inc(sem("vectors_loaded"), 16)
            eng.dma_start(X[:, :, :], x_t).then_inc(sem("x_loaded"), 16)
            eng.dma_start(CTX[:, :, :], ctx_t).then_inc(sem("ctx_loaded"), 16)
            eng.dma_start(CV[:, :], consts[:, 0:NCON1]).then_inc(sem("consts_loaded"), 16)
            for c in range(4):
                eng.dma_start(RAW[c][:, :], stream[c]).then_inc(raw_full[c], 16)
            fours = stream.rearrange("(i j) p n -> j i p n", j=4)
            with eng.Fori(1, N_CHUNKS // 4) as i:
                for j in range(4):
                    eng.wait_ge(lo_done, i * 4 + (j - 3))
                    eng.dma_start(RAW[j][:, :], fours[j, bass.ds(i, 1)].rearrange("o p n -> (o p) n"))\
                       .then_inc(raw_full[j], 16)
            eng.wait_ge(sem("result"), 1)
            eng.dma_start(out, X[:, :, :]).then_inc(sem("stored"), 16)
            eng.wait_ge(sem("stored"), 16)
            for c in range(4):
                eng.wait_ge(raw_full[c], 16 * (N_CHUNKS // 4))

        @block.gpsimd
        def _(eng):
            eng.memset(ONES[:, :], 1.0).then_inc(sem("ones"), 1)

            fours = ada_stream.rearrange("(i j) p n -> j i p n", j=4)
            twos = ada_stream.rearrange("(i j) p n -> j i p n", j=2)

            def load(view, i, slot):
                eng.dma_start(ADA[slot][:, :], view[slot, bass.ds(i, 1)].rearrange("o p n -> (o p) n"))\
                   .then_inc(ada_full[slot], 16)

            for j in range(4):
                load(fours, 0, j)
            with eng.Fori(1, GTL) as i:
                for j in range(4):
                    eng.wait_ge(ada_used, i * 4 + (j - 3))
                    load(fours, i, j)
            for j in range(2):
                eng.wait_ge(ada_used, 4 * GTL + j - 3)
                load(twos, 2 * GTL, j)
            with eng.Fori(1, 2 * (24 - GTL)) as i:
                for j in range(2):
                    eng.wait_ge(ada_fma, i * 8 + 4 * (j - 1))
                    load(twos, i + 2 * GTL, j)

            eng.wait_ge(ada_out, 24 + TAKEN)
            eng.dma_start(PRAW[:, :, :].rearrange("p k t -> p (k t)"), p_t).then_inc(sem("p_loaded"), 16)
            eng.dma_start(POS[:, :], positions).then_inc(sem("positions_loaded"), 16)
            eng.dma_start(CV2[:, :], consts[:, NCON1:NCON]).then_inc(sem("consts2_loaded"), 16)
            eng.memset(MINUS[:, :], -1.0).then_inc(sem("minus_ones"), 1)

            for qt in range(2):
                causal = dict(pattern=[[-1, T]], base=P * qt, channel_multiplier=1, compare_op=ALU.is_ge)
                eng.wait_ge(sem("index_scored"), qt + 1)
                a = Y[:, 13 + qt, :]
                eng.affine_select(out=a, in_=a, fill=NEG, **causal).then_inc(sem("index_masked"), 1)
            for qt in range(2):
                causal = dict(pattern=[[-1, T]], base=P * qt, channel_multiplier=1, compare_op=ALU.is_ge)
                eng.wait_ge(sem("chosen"), qt + 1)
                a = BIASM[:, qt, :]
                eng.affine_select(out=a, in_=a, fill=0.0, **causal).then_inc(sem("chosen_masked"), 1)

        @block.scalar
        def _(act):
            def split(c, base=None, reg=None, step=0):
                n = c if reg is None else c + reg * step
                act.wait_ge(raw_full[c % 4], 16 * (c // 4 + 1) if reg is None else reg * (4 * step) + 16 * (c // 4 + 1))
                if c >= 2:
                    act.wait_ge(pe_chunk, n - 1)
                nc.scalar.activation(HI[c % 2][:, :], RAW[c % 4][:, :], ACT.Copy).then_inc(hi_done, 1)

            pending = [lambda: None]

            def phase(name, n, evac=None, then=None):
                c0, g0 = PH[name]
                evac = evac or (lambda g, reg=None: None)
                stages = evac if isinstance(evac, tuple) else (evac,)

                def stage(s, g, reg):
                    if s < len(stages):
                        stages[s](g, reg)

                def pair(first, reg=None):
                    c = c0 + (0 if first else 8)
                    ri = None if reg is None else reg - 1
                    for j in range(8):
                        split(c + j, reg=ri, step=8)
                        if j == 1 and first:
                            pending[0]()
                        elif 1 <= j < 4 and not first:
                            stage(j - 1, 1, reg - 1)
                        if j >= 5:
                            stage(j - 5, 0, 0 if first else reg)
                if n == 1:
                    for j in range(4):
                        split(c0 + j)
                        if j == 1:
                            pending[0]()
                    last = (0, 0)
                else:
                    pair(True)
                    if n > 3:
                        with act.Fori(1, n // 2) as i:
                            pair(False, i)
                    last = (1, n // 2 - 1)
                    if n % 2:
                        for j in range(4):
                            split(c0 + 4 * (n - 1) + j)
                            if j:
                                stage(j - 1, *last)
                        last = (0, n // 2)

                def rest():
                    for s in range(len(stages)):
                        stage(s, *last)
                    if then:
                        then()
                pending[0] = rest

            def flush():
                pending[0]()
                pending[0] = lambda: None

            def hi_quarter(q, src, dst, ready, done, nth=None):
                act.wait_ge(*since(ready, q + 1 if nth is None else nth))
                nc.scalar.activation(dst[:, 4 * q:4 * q + 4, :], src[:, 4 * q:4 * q + 4, :], ACT.Copy)\
                    .then_inc(step(done)[0], 1)

            def hi_of(*args):
                for q in range(4):
                    hi_quarter(q, *args)

            def squares(name, src, dst, halves=2, ready=None):
                n = src.shape[1] // halves
                for q in range(halves):
                    if ready:
                        act.wait_ge(sem(ready), 2 * q + 2)
                    nc.scalar.activation(dst[:, n * q:n * q + n, :], src[:, n * q:n * q + n, :], ACT.Square)\
                        .then_inc(step(name + "_sq")[0], 1)

            def root(name, w):
                act.wait_ge(*since(name + "_var", 1))
                nc.scalar.activation(RSTD[:, 0:w], RSTD[:, 0:w], ACT.Sqrt).then_inc(step(name + "_std")[0], 1)

            act.wait_ge(sem("vectors_loaded"), 16)
            nc.scalar.activation(SC[:, :], vec("c", 0, 2 * KD), ACT.Silu).then_inc(sem("silu_c"), 1)
            act.wait_ge(sem("x_loaded"), 16)
            squares("nx", X, Y)
            act.wait_ge(sem("ctx_loaded"), 16)
            squares("nc", CTX, SQC)

            def ada_row_copy(ag):
                act.wait_ge(ada_row, ag + 1)
                if ag >= 2:
                    act.wait_ge(ada_sum, ag - 1)
                nc.scalar.activation(FMA[ag % 2][0:2, 0, :], AUX[0:2, 1 + ag % 2, :], ACT.Copy)\
                    .then_inc(ada_row_out, 1)
            ada_row_copy(0)
            ada_row_copy(1)
            root("nx", T)
            root("nc", T)
            for ag in range(2, GTL):
                ada_row_copy(ag)

            def enter():
                for q in range(4):
                    hi_quarter(q, Y, AH, "nx_full", "nx_hi", nth=2 * q + 1)
                    hi_quarter(q, CTX, UH, "nx_full", "nx_hi", nth=2 * q + 2)
            pending[0] = enter
            phase("kv_in", 1, then=None)
            phase("q_in", 1, evac=None)

            def kv_norm_1():
                act.wait_ge(sem("kva"), 1)
                nc.scalar.activation(R2[:, :], R0[:, :], ACT.Square).then_inc(step("nkv_sq")[0], 1)
                root("nkv", 512)
                act.wait_ge(*since("nkv_full", 1))
                nc.scalar.activation(KVH[:, :, :], R0[:, :].rearrange("p (k t) -> p k t", k=2), ACT.Copy)\
                    .then_inc(step("nkv_hi")[0], 1)

            def q_norm_1():
                act.wait_ge(sem("qa"), 1)
                nc.scalar.activation(R2[:, :], R1[:, :], ACT.Square).then_inc(step("nq_sq")[0], 1)
                root("nq", T)
                act.wait_ge(*since("nq_full", 1))
                nc.scalar.activation(QH[:, :, :], R1[:, :].rearrange("p (k t) -> p k t", k=4), ACT.Copy)\
                    .then_inc(step("nq_hi")[0], 1)
            pending[0] = lambda: (kv_norm_1(), q_norm_1())
            phase("conv_in", 6)
            c0 = PH["q_b"][0]
            for j in range(6):
                split(c0 + j)
                if j == 1:
                    flush()
            c0 = PH["w_out"][0]

            scale1 = float(NOPE + ROPE) ** -0.5

            def exp1(u):
                act.wait_ge(sem("max1"), u + 1)
                if u >= 4:
                    act.wait_ge(sem("turned1"), u - 3)
                nc.scalar.activation(PB[u % 4][:, :], AUX[:, u % 2, :], ACT.Exp, bias=COL[:, u % 2:u % 2 + 1],
                                     scale=scale1, accum_out=COL[:, 2 + u % 2:3 + u % 2]).then_inc(sem("exp1"), 1)

            def turned1(u):
                act.wait_ge(sem("turned1"), u + 1)
                if u >= 4:
                    act.wait_ge(acc_full, PH["att1"][1] + u // 2 - 1)
                nc.scalar.activation(PT[u // 2 % 2][:, :, P * (u % 2):P * (u % 2) + P],
                                     AUX[:, 2 + u % 2, :].rearrange("p (k q) -> p k q", k=4), ACT.Copy)\
                    .then_inc(sem("probs1"), 1)

            for u in range(2 * NH1):
                exp1(u)
                if u:
                    turned1(u - 1)
            turned1(2 * NH1 - 1)

            def merge():
                src = [Y[:, 0:4, :], Y[:, 4:8, :], U[:, 0:4, :], U[:, 4:8, :]]

                def root_mix(b):
                    act.wait_ge(sem("mix_var"), b + 1)
                    nc.scalar.activation(MIXV[b], MIXV[b], ACT.Sqrt).then_inc(sem("mix_std"), 1)

                act.wait_ge(sem("att1_done"), 1)
                for b in range(4):
                    nc.scalar.activation(U[:, 16 + 4 * b:20 + 4 * b, :], src[b], ACT.Square)\
                        .then_inc(sem("mix_sq"), 1)
                root_mix(0)
                root_mix(1)
                for b in range(4):
                    act.wait_ge(sem("mix_full"), b + 1)
                    nc.scalar.activation(AH[:, 4 * b:4 * b + 4, :], src[b], ACT.Copy).then_inc(sem("mix_hi"), 1)
                    if b < 2:
                        root_mix(b + 2)
            pending[0] = merge

            def norm(name, dst):
                act.wait_ge(*since(name + "_in", 1))
                squares(name, X, Y)
                root(name, T)
                hi_of(dst, AH, name + "_full", name + "_hi")
            phase("w_out", 4, then=lambda: norm("nf", Y))

            seen = [0]

            def up_evac(parts, base):
                def centre(g, reg, tiles=2):
                    gi = 2 * reg + g
                    n = base[1] + gi
                    act.wait_ge(acc_full, base[0] + gi + 1)
                    if not isinstance(n, int) or n:
                        act.wait_ge(sem("up_done"), n)
                    for t in range(2 * tiles):
                        i = t if tiles == 2 else 2 * t
                        w = gi * 16 + (VEC["ffn_conv"][0] + 16 * base[1] + 4 * i)
                        nc.scalar.activation(Y[:, i, :], ACC[(base[0] + g) % 2][:, t, :], ACT.Identity,
                                             scale=VV[:, bass.ds(w + 1, 1)], bias=VV[:, bass.ds(w + 3, 1)])\
                            .then_inc(sem("up_centre"), 1)

                def silu(g, reg, tiles=2):
                    act.wait_ge(sem("up_conv"), 2 * reg + (g + base[1] + 1))
                    nc.scalar.activation(Y[:, 4:4 + tiles, :], Y[:, 2:2 + tiles, :], ACT.Silu)\
                        .then_inc(sem("up_silu"), 1)

                def hi(g, reg, tiles=2):
                    gi = 2 * reg + g
                    act.wait_ge(sem("up_prod"), gi + (base[1] + 1))
                    nc.scalar.activation(UH[:, bass.ds(gi * 2, tiles), :], Y[:, 6:6 + tiles, :], ACT.Copy)\
                        .then_inc(sem("up_hi"), 1)
                return centre, silu, hi

            for n, (a, b) in enumerate(PARTS):
                ev = up_evac(n, (PH[f"up{n}"][1], a // 2))
                full = (b - a) // 2
                phase(f"up{n}", full, evac=ev)
                if (b - a) % 2:
                    for j in range(2):
                        split(PH[f"up{n}"][0] + 4 * full + j)
                    flush()
                    pending[0] = lambda ev=ev, full=full: [f(full % 2, full // 2, tiles=1) for f in ev]
                if n < 2:
                    phase(f"down{n}", 4)
                else:
                    c0 = PH["down2"][0]
                    for j in range(12):
                        split(c0 + j)
                        if j == 1:
                            flush()
            def enter2():
                norm("n2", X)
                act.wait_ge(sem("angles"), 1)
                for i, (cos, sin) in enumerate(((COS2, SIN2), (COSI, SINI))):
                    r = Y[:, i, :]
                    nc.scalar.activation(cos[:, :], r, ACT.Abs).then_inc(sem("abs_angle"), 1)
                    nc.scalar.activation(sin[:, :], r, ACT.Sin).then_inc(sem("tables"), 1)
                for i, cos in enumerate((COS2, COSI)):
                    act.wait_ge(sem("abs_angle"), 2)
                    nc.scalar.activation(cos[:, :], cos[:, :], ACT.Sin, bias=con("half_pi"), scale=-1.0)\
                        .then_inc(sem("tables"), 1)
            pending[0] = enter2
            c0 = PH["ikw"][0]
            for j in range(2):
                split(c0 + j)
                if j == 1:
                    flush()
            phase("iq", 2)
            flush()

            for u in range(IH):
                act.wait_ge(sem("index_dots"), u + 1)
                if u >= 2:
                    act.wait_ge(sem("index_added"), 2 * (u - 1))
                nc.scalar.activation(R2[:, 512 * (u % 2):512 * (u % 2) + 512].rearrange("p (h t) -> p h t", h=2),
                                     AUX[:, 2 * (u % 2):2 * (u % 2) + 2, 0:T], ACT.Relu,
                                     scale=(ID ** -0.5) * (IH ** -0.5)).then_inc(sem("index_relu"), 1)
            phase("k_a", 1)
            phase("v_a", 1)
            phase("q_a", 4)

            def silu_gate(tag):
                def f():
                    act.wait_ge(sem("gate_" + tag), 1)
                    nc.scalar.activation(U[:, KD:2 * KD, :], U[:, KD:2 * KD, :], ACT.Silu)\
                        .then_inc(sem("silu_" + tag), 1)
                return f
            phase("gate_a", 4, then=silu_gate("a"))
            flush()


            def exp2(h):
                act.wait_ge(sem("max2"), h + 1)
                for qt in range(2):
                    s = PB[h % 4][:, T * qt:T * qt + T]
                    ins = nc.scalar.activation(s, s, ACT.Exp, bias=COL[:, 4 * (h % 2) + qt:4 * (h % 2) + qt + 1],
                                               accum_out=COL[:, 4 * (h % 2) + 2 + qt:4 * (h % 2) + 3 + qt])
                ins.then_inc(sem("exp2"), 1)

            def turned2(h):
                act.wait_ge(sem("turned2"), h + 1)
                if h >= 2:
                    act.wait_ge(acc_full, PH["att2"][1] + h - 1)
                nc.scalar.activation(PT2[h % 2], AUX[:, 2 + h % 2, :].rearrange("p (k q) -> p k q", k=2), ACT.Copy)\
                    .then_inc(sem("probs2"), 1)

            for h in range(NH2):
                exp2(h)
                if h:
                    turned2(h - 1)
            turned2(NH2 - 1)

            def out_split(tag):
                def f():
                    act.wait_ge(sem("att_" + tag), 1)
                    for q in range(4):
                        nc.scalar.activation(AH[:, 4 * q:4 * q + 4, :], U[:, 4 * q:4 * q + 4, :], ACT.Copy)\
                            .then_inc(sem("att_hi_" + tag), 1)
                return f
            pending[0] = out_split("a")

            def layer_norm(i):
                def f():
                    squares(f"ln{i}", X, Y, ready=f"ln{i}_centred")
                    root(f"ln{i}", T)
                    hi_of(X, AH, f"ln{i}_full", f"ln{i}_hi")
                return f

            def embed(i, then):
                def sig():
                    act.wait_ge(sem(f"pgate{i}_out"), 1)
                    nc.scalar.activation(U[:, 0:KD, :], U[:, 0:KD, :], ACT.Sigmoid).then_inc(sem(f"pgate{i}_sig"), 1)
                phase(f"pgate{i}", 4, then=sig)
                c0 = PH[f"ple{i}"][0]
                split(c0)
                split(c0 + 1)
                flush()
                pending[0] = then

            phase("o_a", 4, then=layer_norm(0))
            act.wait_ge(sem("p_loaded"), 16)
            nc.scalar.activation(PTH[:, :, :], PRAW[:, :, :], ACT.Copy).then_inc(sem("p_hi"), 1)
            embed(0, lambda: hi_of(X, AH, "x1_full", "x1_hi"))
            phase("k_b", 1)
            phase("v_b", 1)
            phase("q_bb", 4)
            phase("gate_b", 4, then=silu_gate("b"))
            flush()
            steps3 = [0]

            def chained(ins):
                steps3[0] += 1
                ins.then_inc(sem("act3"), 1)
                act.wait_ge(sem("act3"), steps3[0])

            def log_one_plus(h):
                z, w = ZS[h % 2], PB[h % 4][:, :]
                act.wait_ge(sem("z3"), h + 1)
                if h >= 4:
                    act.wait_ge(acc_full, PH["att3"][1] + h - 3)
                chained(nc.scalar.activation(w, z, ACT.Abs))
                chained(nc.scalar.activation(w, w, ACT.Exp, scale=-1.0))
                nc.scalar.activation(w, w, ACT.Ln, bias=1.0).then_inc(sem("ln3"), 1)

            log_one_plus(0)
            for h in range(NH2):
                if h + 1 < NH2:
                    log_one_plus(h + 1)
                act.wait_ge(sem("w3"), h + 1)
                nc.scalar.activation(PB[h % 4][:, :], ZS[h % 2], ACT.Exp).then_inc(sem("exp3"), 1)
            pending[0] = out_split("b")
            phase("o_b", 4, then=layer_norm(1))
            embed(1, lambda: None)

        @block.vector
        def _(dve):
            V = nc.vector
            chain = [0]

            def link(ins):
                chain[0] += 1
                ins.then_inc(sem("dve_chain"), 1)
                dve.wait_ge(sem("dve_chain"), chain[0])

            def split(c, reg=None, step=0):
                n = c if reg is None else c + reg * step
                dve.wait_ge(hi_done, n + 1)
                if c >= 2:
                    dve.wait_ge(pe_chunk, n - 1)
                V.tensor_tensor(LO[c % 2][:, :], RAW[c % 4][:, :], HI[c % 2][:, :].bitcast(F32), ALU.subtract)\
                    .then_inc(lo_done, 1)

            def take(g):
                dve.wait_ge(acc_full, g + 1)

            def ada_chunk(ag, j, acc, n0, slot, full, first_wait=None):
                dve.wait_ge(ada_full[slot], full)
                for k in range(4):
                    a = acc[:, k % 2, :]
                    w = ADA[slot][:, 512 * k:512 * k + 512]
                    s = SC[:, 4 * j + k:4 * j + k + 1]
                    if j == 0 and k < 2:
                        if k == 0:
                            dve.wait_ge(ada_sum, first_wait)
                        V.tensor_scalar(a, w, s, None, ALU.mult).then_inc(ada_fma, 1)
                    else:
                        dve.wait_ge(ada_fma, n0 + (k - 1))
                        V.scalar_tensor_tensor(out=a, in0=w, scalar=s, in1=a, op0=ALU.mult, op1=ALU.add)\
                            .then_inc(ada_fma, 1)

            def ada_take(ag):
                dve.wait_ge(ada_sum, ag + 1)
                V.tensor_tensor(MOD[:, bass.ds(ag * 4, 4)], AUX[:, 3, 0:4],
                                VV[:, bass.ds(ag * 4 + VEC["b_ada"][0], 4)], ALU.add).then_inc(ada_out, 1)

            pending = [lambda: None]

            def carried(name, j, g, reg):
                if name not in CARRY:
                    return
                first, per = CARRY[name]
                if per == 2:
                    ag = first + (reg if reg is not None else 0)
                    jj = 2 * g + j
                    if j >= 2:
                        return
                    n0 = (ag - GTL) * 16 + 4 * jj
                    full = ag * 32 + 16 * (jj // 2 + 1 - GTL)
                    ada_chunk(ag, jj, FMA[0], n0, jj % 2, full,
                              first_wait=ag if jj == 0 else None)
                else:
                    ag = first + g + (2 * reg if reg is not None else 0)
                    n0 = (ag - GTL) * 16 + 4 * j
                    full = ag * 32 + 16 * (j // 2 + 1 - GTL)
                    ada_chunk(ag, j, FMA[(first + g) % 2], n0, j % 2, full,
                              first_wait=(ag - 1) if j == 0 else None)

            def carried_take(name, g, reg):
                if name not in CARRY:
                    return
                first, per = CARRY[name]
                if per == 2:
                    if g == 0:
                        return
                    ag = reg + first
                    if isinstance(reg, int):
                        ag = first + reg
                else:
                    ag = 2 * reg + (first + g)
                ada_take(ag)

            def phase(name, n, evac, then=None):
                c0, g0 = PH[name]
                stages = evac if isinstance(evac, tuple) else (evac,)

                def stage(s, g, reg):
                    if s < len(stages):
                        stages[s](g, reg)

                def pair(first, reg=None):
                    c = c0 + (0 if first else 8)
                    ri = None if reg is None else reg - 1
                    for j in range(8):
                        split(c + j, reg=ri, step=8)
                        carried(name, j % 4, j // 4, reg)
                        if j == 1 and first:
                            pending[0]()
                        elif 1 <= j < 4 and not first:
                            stage(j - 1, 1, reg - 1)
                        if j >= 5:
                            stage(j - 5, 0, 0 if first else reg)
                        if j == 1 and not first:
                            carried_take(name, 1, reg - 1)
                        if j == 5:
                            carried_take(name, 0, 0 if first else reg)
                if n == 1:
                    for j in range(4):
                        split(c0 + j)
                        carried(name, j, 0, None)
                        if j == 1:
                            pending[0]()
                    last = (0, 0)
                else:
                    pair(True)
                    if n > 3:
                        with dve.Fori(1, n // 2) as i:
                            pair(False, i)
                    last = (1, n // 2 - 1)
                    if n % 2:
                        for j in range(4):
                            split(c0 + 4 * (n - 1) + j)
                            if j:
                                stage(j - 1, *last)
                        last = (0, n // 2)

                def rest():
                    for s in range(len(stages)):
                        stage(s, *last)
                    carried_take(name, *last)
                    if then:
                        then()
                pending[0] = rest

            def flush():
                pending[0]()
                pending[0] = lambda: None

            def copy_out(name, dst, d0, n=4):
                g0 = PH[name][1]

                def evac(g, reg):
                    gi = 2 * reg + g
                    take(g0 + gi)
                    V.tensor_copy(dst[:, bass.ds(gi * 4 + d0, n), :], ACC[(g0 + g) % 2][:, 0:n, :])\
                        .then_inc(acc_free, 1)
                return evac

            def total(name, src, w, order="p k t -> p t k", halves=2):
                dve.wait_ge(*since(name + "_sq", halves))
                V.tensor_reduce(RSTD[:, 0:w], src.rearrange(order), AX.X, ALU.add).then_inc(step(name + "_ss")[0], 1)

            def variance(name, w, n, eps):
                dve.wait_ge(*since(name + "_tot", 1))
                V.tensor_scalar(RSTD[:, 0:w], AUX[:, 0, 0:w], 1.0 / n, eps, ALU.mult, ALU.add)\
                    .then_inc(step(name + "_var")[0], 1)
                dve.wait_ge(*since(name + "_std", 1))
                link(V.reciprocal(RSTD[:, 0:w], RSTD[:, 0:w]))

            def wide_bcast(a, n):
                return a.unsqueeze(1).to_broadcast([P, n, a.shape[-1]])

            def lo_quarter(q, src, dst_hi, dst_lo, hi_sem, done, nth=None):
                s = slice(4 * q, 4 * q + 4)
                dve.wait_ge(*since(hi_sem, q + 1 if nth is None else nth))
                V.tensor_tensor(dst_lo[:, s, :], src[:, s, :], dst_hi[:, s, :].bitcast(F32), ALU.subtract)\
                    .then_inc(sem(done), 1)

            def lo_of(*args):
                for q in range(4):
                    lo_quarter(q, *args)

            def normed(name, src, dst, scale, shift, done):
                for q in range(4):
                    s = slice(4 * q, 4 * q + 4)
                    link(V.tensor_tensor(dst[:, s, :], src[:, s, :], wide_bcast(RSTD[:, 0:T], 4), ALU.mult))
                    for k in range(4 * q, 4 * q + 4):
                        ins = V.tensor_scalar(dst[:, k, :], dst[:, k, :], scale(k), None, ALU.mult) if shift is None \
                            else V.tensor_scalar(dst[:, k, :], dst[:, k, :], scale(k), shift(k), ALU.mult, ALU.add)
                    ins.then_inc(step(name + "_full")[0], 1)
                    if q:
                        lo_quarter(q - 1, dst, AH, AL, name + "_hi", done)
                lo_quarter(3, dst, AH, AL, name + "_hi", done)

            total("nx", Y[:, :, :], T)
            variance("nx", T, D, EPS)
            link(V.tensor_tensor(Y[:, :, :], X[:, :, :], wide_bcast(RSTD[:, 0:T], KD), ALU.mult))
            total("nc", SQC[:, :, :], T)
            variance("nc", T, D, EPS)
            link(V.tensor_tensor(CTX[:, :, :], CTX[:, :, :], wide_bcast(RSTD[:, 0:T], KD), ALU.mult))
            dve.wait_ge(ada_sum, GTL)
            for v, m in enumerate((MOD, MODC)):
                V.tensor_tensor(m[:, 0:4 * GTL], AUX[:, 3, 0:8 * GTL].rearrange("p (n v) -> p v n", v=2)[:, v, :],
                                vec("b_ada", 0, 4 * GTL), ALU.add).then_inc(ada_out, 1)
            dve.wait_ge(ada_out, 2)
            dve.wait_ge(sem("silu_c"), 1)
            for k, m in ((0, MOD), (KD, MODC)):
                link(V.tensor_scalar(SCL[:, k:k + KD], m[:, KD:2 * KD], 1.0, None, ALU.add))
                link(V.tensor_tensor(SCL[:, k:k + KD], SCL[:, k:k + KD], vec("g_mix_norm", 0, KD), ALU.mult))

            def enter():
                for q in range(4):
                    for name, a, m, s0 in (("nx", Y, MOD, 0), ("nc", CTX, MODC, KD)):
                        for k in range(4 * q, 4 * q + 4):
                            ins = V.tensor_scalar(a[:, k, :], a[:, k, :], SCL[:, s0 + k:s0 + k + 1], m[:, k:k + 1],
                                                  ALU.mult, ALU.add)
                        ins.then_inc(step(name + "_full")[0], 1)
                    if q:
                        lo_pair(q - 1)
                lo_pair(3)

            def lo_pair(q):
                lo_quarter(q, Y, AH, AL, "nx_hi", "in_ready", nth=2 * q + 1)
                lo_quarter(q, CTX, UH, UL, "nx_hi", "ctx_ready", nth=2 * q + 2)
            pending[0] = enter

            def kv_evac(g, reg):
                take(PH["kv_in"][1])
                a = R0[:, :].rearrange("p (k t) -> p k t", k=2)
                V.tensor_copy(a[:, :, 0:T], ACC[0][:, 0:2, :])
                V.tensor_copy(a[:, :, T:512], AUX[:, 0, :].rearrange("p (k t) -> p k t", k=2)).then_inc(sem("kva"), 1)
                V.tensor_copy(KR[:, T:512], AUX[:, 1, 0:T])
                V.tensor_copy(KR[:, 0:T], ACC[0][:, 2, :]).then_inc(sem("kr_copied"), 1)
                V.engine_nop().then_inc(acc_free, 1)

            def q_evac(g, reg):
                g0 = PH["q_in"][1]
                take(g0)
                V.tensor_copy(R1[:, :].rearrange("p (k t) -> p k t", k=4), ACC[g0 % 2][:, :, :])\
                    .then_inc(sem("qa"), 1)
                V.engine_nop().then_inc(acc_free, 1)

            def small_norms():
                total("nkv", R2[:, :].rearrange("p (k t) -> p k t", k=2), 512, halves=1)
                variance("nkv", 512, KV_RANK, EPS)
                for k in range(2):
                    a = R0[:, 512 * k:512 * k + 512]
                    ins = V.scalar_tensor_tensor(out=a, in0=a, scalar=vec("g_kv_a", k), in1=RSTD[:, :],
                                                 op0=ALU.mult, op1=ALU.mult)
                ins.then_inc(step("nkv_full")[0], 1)
                dve.wait_ge(*since("nkv_hi", 1))
                V.tensor_tensor(KVL[:, :, :], R0[:, :].rearrange("p (k t) -> p k t", k=2),
                                KVH[:, :, :].bitcast(F32), ALU.subtract).then_inc(sem("kv_ready"), 1)
                total("nq", R2[:, :].rearrange("p (k t) -> p k t", k=4), T, halves=1)
                variance("nq", T, Q_RANK, EPS)
                for k in range(4):
                    a = R1[:, T * k:T * k + T]
                    ins = V.scalar_tensor_tensor(out=a, in0=a, scalar=vec("g_q_a", k), in1=RSTD[:, 0:T],
                                                 op0=ALU.mult, op1=ALU.mult)
                ins.then_inc(step("nq_full")[0], 1)
                dve.wait_ge(*since("nq_hi", 1))
                V.tensor_tensor(QL[:, :, :], R1[:, :].rearrange("p (k t) -> p k t", k=4),
                                QH[:, :, :].bitcast(F32), ALU.subtract).then_inc(sem("q_ready"), 1)
                dve.wait_ge(sem("kr_rot"), 1)
                rope(KR[:, 0:T], AUX[:, 1, 0:T], con("cos1"), con("sin1"), R2[:, 0:T], R2[:, T:2 * T])

            def rope(x, rotated, cos, sin, w0, w1):
                link(V.tensor_tensor(w0, rotated, sin, ALU.mult))
                link(V.tensor_tensor(w1, x, cos, ALU.mult))
                link(V.tensor_tensor(x, w0, w1, ALU.add))

            phase("kv_in", 1, evac=kv_evac)
            phase("q_in", 1, evac=q_evac, then=small_norms)
            phase("conv_in", 6, evac=copy_out("conv_in", U, 0))

            def conv_branch():
                dve.wait_ge(acc_free, PH["q_b"][1])
                for k in range(2):
                    s = slice(8 + 4 * k, 12 + 4 * k)
                    link(V.tensor_tensor(U[:, s, :], U[:, s, :], U[:, 16 + 4 * k:20 + 4 * k, :], ALU.mult))
                w = VEC["conv"][0]
                col = lambda k, i: VV[:, w + 4 * k + i:w + 4 * k + i + 1]
                for k in range(8):
                    ins = V.tensor_scalar(U[:, 24 + k, :], U[:, 8 + k, :], col(k, 1), col(k, 3), ALU.mult, ALU.add)
                link(ins)
                for k in range(8):
                    o = U[:, 24 + k, 1:T]
                    ins = V.scalar_tensor_tensor(out=o, in0=U[:, 8 + k, 0:T - 1], scalar=col(k, 0), in1=o,
                                                 op0=ALU.mult, op1=ALU.add)
                link(ins)
                for k in range(8):
                    o = U[:, 24 + k, 0:T - 1]
                    ins = V.scalar_tensor_tensor(out=o, in0=U[:, 8 + k, 1:T], scalar=col(k, 2), in1=o,
                                                 op0=ALU.mult, op1=ALU.add)
                link(ins)
                link(V.tensor_tensor(U[:, 0:8, :], U[:, 0:8, :], U[:, 24:32, :], ALU.mult))

            c0, g0 = PH["q_b"]
            for j in range(6):
                split(c0 + j)
                if j == 1:
                    flush()
                    conv_branch()
                if 2 <= j < 4 or j == 4:
                    pair = j - 2
                    take(g0 + pair)
                    V.tensor_copy(QT1[:, 2 * pair:2 * pair + 2, :], ACC[(g0 + pair) % 2][:, 0:2, :])
                    V.tensor_copy(QT1[:, 8 + pair, :], ACC[(g0 + pair) % 2][:, 2, :]).then_inc(acc_free, 1)
            take(g0 + 3)
            V.tensor_copy(QT1[:, 6:8, :], ACC[(g0 + 3) % 2][:, 0:2, :])
            V.tensor_copy(QT1[:, 11, :], ACC[(g0 + 3) % 2][:, 2, :]).then_inc(acc_free, 1)
            V.engine_nop().then_inc(sem("qt1"), 1)
            g0 = PH["kv_b"][1]
            for i in range(4):
                take(g0 + i)
                V.tensor_copy(KN1[:, 2 * i:2 * i + 2, :].rearrange("p a b -> p (a b)"),
                              ACC[(g0 + i) % 2][:, :, :].rearrange("p a b -> p (a b)")).then_inc(acc_free, 1)
            for i in range(4):
                take(g0 + 4 + i)
                V.tensor_copy(V1[:, i, :], ACC[(g0 + i) % 2][:, :, :].rearrange("p a b -> p (a b)"))\
                    .then_inc(acc_free, 1)
            dve.wait_ge(sem("q_rot"), 1)
            rope(QT1[:, 8:12, :], AUX[:, 0:2, :].rearrange("p a (b t) -> p (a b) t", t=T),
                 wide_bcast(con("cos1"), 4), wide_bcast(con("sin1"), 4),
                 Y[:, 0:4, :], Y[:, 4:8, :])
            V.engine_nop().then_inc(sem("att1_in"), 1)

            g0 = PH["att1"][1]
            scale1 = float(NOPE + ROPE) ** -0.5

            def weighted(u):
                dve.wait_ge(sem("exp1"), u + 1)
                link(V.reciprocal(COL[:, 4 + u % 2:5 + u % 2], COL[:, 2 + u % 2:3 + u % 2]))
                V.tensor_scalar(PB[u % 4][:, :], PB[u % 4][:, :], COL[:, 4 + u % 2:5 + u % 2], None, ALU.mult)\
                    .then_inc(sem("normed1"), 1)

            def head_out(h):
                take(g0 + h)
                V.tensor_copy(Y[:, h, :], ACC[(g0 + h) % 2][:, 0, :]).then_inc(acc_free, 1)

            for u in range(2 * NH1):
                dve.wait_ge(sem("scores1"), u + 1)
                link(V.tensor_reduce(COL[:, 6 + u % 2:7 + u % 2], AUX[:, u % 2, :], AX.X, ALU.max))
                V.tensor_scalar(COL[:, u % 2:u % 2 + 1], COL[:, 6 + u % 2:7 + u % 2], -scale1, None, ALU.mult)\
                    .then_inc(sem("max1"), 1)
                if u:
                    weighted(u - 1)
                if u % 2 == 0 and u >= 4:
                    head_out(u // 2 - 2)
            weighted(2 * NH1 - 1)
            head_out(NH1 - 2)
            head_out(NH1 - 1)
            V.engine_nop().then_inc(sem("att1_done"), 1)

            def merge():
                src = [Y[:, 0:4, :], Y[:, 4:8, :], U[:, 0:4, :], U[:, 4:8, :]]

                def var_mix(b):
                    dve.wait_ge(sem("mix_tot"), b + 1)
                    a = 2 * (b % 2)
                    V.tensor_scalar(MIXV[b].rearrange("p a b -> p (a b)"),
                                    AUX[:, a:a + 2, :].rearrange("p a b -> p (a b)"), 1.0 / P, EPS,
                                    ALU.mult, ALU.add).then_inc(sem("mix_var"), 1)

                def lo_mix(b):
                    dve.wait_ge(sem("mix_hi"), b + 1)
                    V.tensor_tensor(AL[:, 4 * b:4 * b + 4, :], src[b], AH[:, 4 * b:4 * b + 4, :].bitcast(F32),
                                    ALU.subtract).then_inc(sem("mix_ready"), 1)

                var_mix(0)
                var_mix(1)
                for b in range(4):
                    dve.wait_ge(sem("mix_std"), b + 1)
                    link(V.reciprocal(MIXV[b], MIXV[b]))
                    for k in range(4):
                        ins = V.scalar_tensor_tensor(out=src[b][:, k, :], in0=src[b][:, k, :],
                                                     scalar=vec("g_mix_out", 4 * b + k), in1=MIXV[b][:, k, :],
                                                     op0=ALU.mult, op1=ALU.mult)
                    ins.then_inc(sem("mix_full"), 1)
                    if b < 2:
                        var_mix(b + 2)
                    if b:
                        lo_mix(b - 1)
                lo_mix(3)
            pending[0] = merge

            def residual(name, gate):
                g0 = PH[name][1]

                def evac(g, reg):
                    gi = 2 * reg + g
                    take(g0 + gi)
                    for t in range(4):
                        x = X[:, bass.ds(gi * 4 + t, 1), :].rearrange("p a t -> p (a t)")
                        ins = V.scalar_tensor_tensor(out=x, in0=ACC[(g0 + g) % 2][:, t, :],
                                                     scalar=MOD[:, bass.ds(gi * 4 + (gate + t), 1)], in1=x,
                                                     op0=ALU.mult, op1=ALU.add)
                    ins.then_inc(acc_free, 1)
                return evac

            def ffn_in():
                g_end = PH["up0"][1]
                dve.wait_ge(acc_free, g_end)
                V.engine_nop().then_inc(sem("nf_in"), 1)
                dve.wait_ge(ada_out, 20 + TAKEN)
                link(V.tensor_scalar(SCL[:, 0:KD], MOD[:, 4 * KD:5 * KD], 1.0, None, ALU.add))
                link(V.tensor_tensor(SCL[:, 0:KD], SCL[:, 0:KD], vec("g_ffn_norm", 0, KD), ALU.mult))
                total("nf", Y[:, :, :], T)
                variance("nf", T, D, EPS)
                normed("nf", X, Y, lambda k: SCL[:, k:k + 1], lambda k: MOD[:, 3 * KD + k:3 * KD + k + 1],
                       "ffn_ready")
            phase("w_out", 4, evac=residual("w_out", 2 * KD), then=ffn_in)

            def up_evac(base):
                def taps(g, reg, tiles=2):
                    gi = 2 * reg + g
                    n = base[1] + gi
                    acc = ACC[(base[0] + g) % 2]
                    take(base[0] + gi)
                    dve.wait_ge(sem("up_centre"), n * 4 + 2 * tiles)
                    order = [(t, t if tiles == 2 else 2 * t) for t in range(2 * tiles)]
                    for t, i in order:
                        w = gi * 16 + (VEC["ffn_conv"][0] + 16 * base[1] + 4 * i)
                        ins = V.scalar_tensor_tensor(out=Y[:, i, 1:T], in0=acc[:, t, 0:T - 1],
                                                     scalar=VV[:, bass.ds(w, 1)], in1=Y[:, i, 1:T],
                                                     op0=ALU.mult, op1=ALU.add)
                    ins.then_inc(sem("up_left"), 1)
                    dve.wait_ge(sem("up_left"), n + 1)
                    for t, i in order:
                        w = gi * 16 + (VEC["ffn_conv"][0] + 16 * base[1] + 4 * i)
                        ins = V.scalar_tensor_tensor(out=Y[:, i, 0:T - 1], in0=acc[:, t, 1:T],
                                                     scalar=VV[:, bass.ds(w + 2, 1)], in1=Y[:, i, 0:T - 1],
                                                     op0=ALU.mult, op1=ALU.add)
                    ins.then_inc(sem("up_conv"), 1)
                    V.engine_nop().then_inc(acc_free, 1)

                def product(g, reg, tiles=2):
                    dve.wait_ge(sem("up_silu"), 2 * reg + (g + base[1] + 1))
                    V.tensor_tensor(Y[:, 6:6 + tiles, :], Y[:, 0:tiles, :], Y[:, 4:4 + tiles, :], ALU.mult)\
                        .then_inc(sem("up_prod"), 1)

                def lo(g, reg, tiles=2):
                    gi = 2 * reg + g
                    dve.wait_ge(sem("up_hi"), gi + (base[1] + 1))
                    V.tensor_tensor(UL[:, bass.ds(gi * 2, tiles), :], Y[:, 6:6 + tiles, :],
                                    UH[:, bass.ds(gi * 2, tiles), :].bitcast(F32), ALU.subtract)\
                        .then_inc(sem("up_done"), 1)
                return taps, product, lo

            for n, (a, b) in enumerate(PARTS):
                ev = up_evac((PH[f"up{n}"][1], a // 2))
                full = (b - a) // 2
                phase(f"up{n}", full, evac=ev)
                if (b - a) % 2:
                    for j in range(2):
                        split(PH[f"up{n}"][0] + 4 * full + j)
                    flush()
                    pending[0] = lambda ev=ev, full=full: [f(full % 2, full // 2, tiles=1) for f in ev]
                res = residual(f"down{n}", 5 * KD)
                if n < 2:
                    phase(f"down{n}", 4, evac=res)
                else:
                    c0 = PH["down2"][0]
                    for j in range(12):
                        split(c0 + j)
                        if j == 1:
                            flush()
                        if j % 3 == 1 and j > 1:
                            g = j // 3 - 1
                            res(g % 2, g // 2)

            def angles():
                dve.wait_ge(sem("positions_loaded"), 16)
                link(V.tensor_copy(R2[:, 0:T], POS[:, :]))
                for i, inv in enumerate(("inv2", "invi")):
                    r, n, m = Y[:, i, :], R2[:, 2 * T:3 * T], R2[:, 3 * T:4 * T]
                    link(V.tensor_scalar(r, R2[:, 0:T], con(inv), None, ALU.mult))
                    link(V.tensor_scalar(n, r, 1.0 / (2 * np.pi), 12582912.0, ALU.mult, ALU.add))
                    link(V.tensor_scalar(n, n, -12582912.0, None, ALU.add))
                    for part in (6.28125, 1.9350051879882812e-03, 3.0199157663446332e-07):
                        link(V.scalar_tensor_tensor(out=r, in0=n, scalar=-part, in1=r, op0=ALU.mult, op1=ALU.add))
                    link(V.tensor_scalar(r, r, 3.141592, -3.141592, ALU.min, ALU.max))
                V.engine_nop().then_inc(sem("angles"), 1)

            def enter2():
                dve.wait_ge(acc_free, PH["ikw"][1])
                V.engine_nop().then_inc(sem("n2_in"), 1)
                total("n2", Y[:, :, :], T)
                variance("n2", T, D, EPS)
                normed("n2", X, X, lambda k: vec("g_final", k), None, "a_ready")
                angles()
            c0, g0 = PH["ikw"]
            last = PH["down2"][1] + 3
            pending[0] = lambda: (residual("down2", 5 * KD)(1, 1), enter2())
            for j in range(2):
                split(c0 + j)
                if j == 1:
                    flush()

            def ikw_evac():
                take(g0)
                V.tensor_copy(Y[:, 12, :], ACC[g0 % 2][:, 0, :])
                V.tensor_copy(IW[:, :, :], ACC[g0 % 2][:, 2, 0:32].rearrange("p (a b) -> p a b", a=2))\
                    .then_inc(acc_free, 1)
                V.engine_nop().then_inc(sem("ik"), 1)
            pending[0] = ikw_evac
            phase("iq", 2, evac=copy_out("iq", Y, 4))
            flush()
            V.engine_nop().then_inc(sem("iq"), 1)
            dve.wait_ge(sem("tables"), 4)
            for b in range(3):
                n = 4 if b < 2 else 1
                dve.wait_ge(sem("index_rot"), b + 1)
                x = Y[:, 4 + 4 * b:4 + 4 * b + n, :]
                w = R1[:, 0:n * T].rearrange("p (a t) -> p a t", t=T)
                v = R2[:, 0:n * T].rearrange("p (a t) -> p a t", t=T)
                rot = AUX[:, 0:2, :].rearrange("p a (b t) -> p (a b) t", t=T)[:, 0:n, :] if b != 1 else \
                    AUX[:, 2:4, :].rearrange("p a (b t) -> p (a b) t", t=T)
                rope(x, rot, wide_bcast(COSI[:, :], n), wide_bcast(SINI[:, :], n), w, v)
                V.engine_nop().then_inc(sem("index_in"), 1)
            for u in range(IH):
                qt, h = u // 8, 2 * (u % 8)
                dve.wait_ge(sem("index_relu"), u + 1)
                for i in range(2):
                    acc = Y[:, 13 + qt, :] if i == 0 else R1[:, T * qt:T * qt + T]
                    x = R2[:, 512 * (u % 2) + T * i:512 * (u % 2) + T * i + T]
                    s = IW[:, qt, h + i:h + i + 1]
                    if h == 0:
                        V.tensor_scalar(acc, x, s, None, ALU.mult).then_inc(sem("index_added"), 1)
                    else:
                        dve.wait_ge(sem("index_added"), 2 * u + i - 1)
                        V.scalar_tensor_tensor(out=acc, in0=x, scalar=s, in1=acc, op0=ALU.mult, op1=ALU.add)\
                            .then_inc(sem("index_added"), 1)
                if h == 14:
                    dve.wait_ge(sem("index_added"), 2 * u + 2)
                    V.tensor_tensor(Y[:, 13 + qt, :], Y[:, 13 + qt, :], R1[:, T * qt:T * qt + T], ALU.add)\
                        .then_inc(sem("index_scored"), 1)
            for qt in range(2):
                dve.wait_ge(sem("index_masked"), qt + 1)
                work = Y[:, 13 + qt, :]
                for r in range(TOPK // 8):
                    link(V.max(COL[:, 48:56], work))
                    link(V.match_replace(out=work, in_to_replace=COL[:, 48:56], in_values=work, imm_value=MARK))
                V.tensor_scalar(BIASM[:, qt, :], work, MARK, BIG, ALU.is_equal, ALU.mult).then_inc(sem("chosen"), 1)
            for qt in range(2):
                dve.wait_ge(sem("chosen_masked"), qt + 1)
                link(V.tensor_scalar(BIASM[:, qt, :], BIASM[:, qt, :], -BIG, None, ALU.add))

            def token_major(name, dst):
                g0 = PH[name][1]

                def evac(g, reg):
                    take(g0)
                    V.tensor_copy(dst, ACC[g0 % 2][:, :, :].rearrange("p a b -> p (a b)")).then_inc(acc_free, 1)
                return evac

            phase("k_a", 1, evac=copy_out("k_a", Y, 0))
            phase("v_a", 1, evac=token_major("v_a", R0[:, :]))
            phase("q_a", 4, evac=copy_out("q_a", U, 0))

            def gate_then(tag):
                def f():
                    dve.wait_ge(acc_free, PH["att2" if tag == "a" else "att3"][1])
                    V.engine_nop().then_inc(sem("gate_" + tag), 1)
                return f
            phase("gate_a", 4, evac=copy_out("gate_a", U, KD), then=gate_then("a"))
            flush()
            for b in range(5):
                x = Y[:, 0:4, :] if b == 0 else U[:, 4 * b - 4:4 * b, :]
                dve.wait_ge(sem("a_rot"), b + 1)
                a = 2 * (b % 2)
                rope(x, AUX[:, a:a + 2, :].rearrange("p a (b t) -> p (a b) t", t=T), wide_bcast(COS2[:, :], 4),
                     wide_bcast(SIN2[:, :], 4), R1[:, :].rearrange("p (a t) -> p a t", t=T),
                     R2[:, :].rearrange("p (a t) -> p a t", t=T))
                V.engine_nop().then_inc(sem("a_in"), 1)

            g0 = PH["att2"][1]

            def weighted2(h):
                dve.wait_ge(sem("exp2"), h + 1)
                link(V.reciprocal(COL[:, 16 + 2 * (h % 2):18 + 2 * (h % 2)],
                                  COL[:, 4 * (h % 2) + 2:4 * (h % 2) + 4]))
                for qt in range(2):
                    s = PB[h % 4][:, T * qt:T * qt + T]
                    k = 16 + 2 * (h % 2) + qt
                    ins = V.tensor_scalar(s, s, COL[:, k:k + 1], None, ALU.mult)
                ins.then_inc(sem("normed2"), 1)

            def gated(h, g0, tag):
                if h == 0:
                    dve.wait_ge(sem("silu_" + tag), 1)
                take(g0 + h)
                V.tensor_tensor(U[:, h, :], ACC[(g0 + h) % 2][:, 0, :], U[:, KD + h, :], ALU.mult)\
                    .then_inc(acc_free, 1)

            for h in range(NH2):
                dve.wait_ge(sem("scores2"), h + 1)
                if h >= 4:
                    dve.wait_ge(sem("turned2"), h - 3)
                link(V.scalar_tensor_tensor(out=PB[h % 4][:, :], in0=AUX[:, h % 2, :], scalar=HD ** -0.5,
                                            in1=BIASM[:, :, :].rearrange("p a t -> p (a t)"),
                                            op0=ALU.mult, op1=ALU.add))
                k = 20 + 2 * (h % 2)
                link(V.tensor_reduce(COL[:, k:k + 2], PB[h % 4][:, :].rearrange("p (a t) -> p a t", a=2),
                                     AX.X, ALU.max))
                V.tensor_scalar(COL[:, 4 * (h % 2):4 * (h % 2) + 2], COL[:, k:k + 2], -1.0, None, ALU.mult)\
                    .then_inc(sem("max2"), 1)
                if h:
                    weighted2(h - 1)
                if h >= 3:
                    gated(h - 3, g0, "a")
            weighted2(NH2 - 1)
            gated(NH2 - 3, g0, "a")
            gated(NH2 - 2, g0, "a")
            gated(NH2 - 1, g0, "a")

            def out_split(tag, nxt):
                def f():
                    dve.wait_ge(acc_free, PH[nxt][1])
                    V.engine_nop().then_inc(sem("att_" + tag), 1)
                    lo_of(U, AH, AL, "att_hi_" + tag, "att_ready_" + tag)
                return f
            pending[0] = out_split("a", "o_a")

            def add_alpha(name):
                g0 = PH[name][1]

                def evac(g, reg):
                    gi = 2 * reg + g
                    take(g0 + gi)
                    x = X[:, bass.ds(gi * 4, 4), :]
                    V.scalar_tensor_tensor(out=x, in0=x, scalar=ALPHA, in1=ACC[(g0 + g) % 2][:, :, :],
                                           op0=ALU.mult, op1=ALU.add).then_inc(acc_free, 1)
                return evac

            def layer_norm(i):
                def f():
                    n = f"ln{i}"
                    dve.wait_ge(acc_free, PH[f"pgate{i}"][1])
                    link(V.tensor_reduce(RSTD[:, 0:T], X[:, :, :].rearrange("p k t -> p t k"), AX.X, ALU.add))
                    V.engine_nop().then_inc(sem(n + "_sum"), 1)
                    dve.wait_ge(sem(n + "_mean"), 1)
                    link(V.tensor_scalar(RSTD[:, T:2 * T], AUX[:, 1, 0:T], 1.0 / D, None, ALU.mult))
                    for q in range(4):
                        s = slice(4 * q, 4 * q + 4)
                        V.tensor_tensor(X[:, s, :], X[:, s, :], wide_bcast(RSTD[:, T:2 * T], 4), ALU.subtract)\
                            .then_inc(sem(n + "_centred"), 1)
                    total(n, Y[:, :, :], T)
                    variance(n, T, D, LN_EPS)
                    normed(n, X, X, lambda k: vec("ln_g", KD * i + k), lambda k: vec("ln_b", KD * i + k),
                           n + "_ready")
                return f

            phase("o_a", 4, evac=add_alpha("o_a"), then=layer_norm(0))
            dve.wait_ge(sem("p_hi"), 1)
            V.tensor_tensor(PTL[:, :, :], PRAW[:, :, :], PTH[:, :, :].bitcast(F32),
                            ALU.subtract).then_inc(sem("p_ready"), 1)

            def embed(i, then):
                def gate_out():
                    dve.wait_ge(acc_free, PH[f"ple{i}"][1])
                    V.engine_nop().then_inc(sem(f"pgate{i}_out"), 1)
                phase(f"pgate{i}", 4, evac=copy_out(f"pgate{i}", U, 0), then=gate_out)
                c0, g0 = PH[f"ple{i}"]
                split(c0)
                split(c0 + 1)
                flush()

                def ple():
                    dve.wait_ge(sem(f"pgate{i}_sig"), 1)
                    for g in range(4):
                        take(g0 + g)
                        s = slice(4 * g, 4 * g + 4)
                        V.tensor_tensor(U[:, s, :], U[:, s, :], ACC[(g0 + g) % 2][:, :, :], ALU.mult)\
                            .then_inc(acc_free, 1)
                    for g in range(4):
                        dve.wait_ge(acc_free, g0 + g + 1)
                        s = slice(4 * g, 4 * g + 4)
                        V.tensor_tensor(X[:, s, :], X[:, s, :], U[:, s, :], ALU.add)\
                            .then_inc(sem("x1_full" if i == 0 else "x2_full"), 1)
                ple()
                pending[0] = then

            embed(0, lambda: lo_of(X, AH, AL, "x1_hi", "b_ready"))
            phase("k_b", 1, evac=copy_out("k_b", Y, 0))
            phase("v_b", 1, evac=token_major("v_b", R0[:, :]))
            phase("q_bb", 4, evac=copy_out("q_bb", U, 0))
            phase("gate_b", 4, evac=copy_out("gate_b", U, KD), then=gate_then("b"))
            flush()
            g0 = PH["att3"][1]
            strict = con("strict")

            def softplus(h):
                dve.wait_ge(sem("ln3"), h + 1)
                V.scalar_tensor_tensor(out=PB[h % 4][:, :], in0=ZS[h % 2], scalar=0.0, in1=PB[h % 4][:, :],
                                       op0=ALU.max, op1=ALU.add).then_inc(sem("sp3"), 1)

            def log_weight(h):
                dve.wait_ge(sem("suffix3"), h + 1)
                V.tensor_tensor(ZS[h % 2], ZS[h % 2], AUX[:, 2 + h % 2, :], ALU.add).then_inc(sem("w3"), 1)

            def masked_scores(h):
                dve.wait_ge(sem("scores3"), h + 1)
                z = ZS[h % 2]
                if h >= 2:
                    dve.wait_ge(sem("exp3"), h - 1)
                V.scalar_tensor_tensor(out=z[:, 0:P], in0=AUX[:, h % 2, 0:P], scalar=HD ** -0.5, in1=strict,
                                       op0=ALU.mult, op1=ALU.add)
                V.tensor_scalar(z[:, P:T], AUX[:, h % 2, P:T], HD ** -0.5, None, ALU.mult)
                V.tensor_scalar(z[:, T:T + P], AUX[:, h % 2, T:T + P], HD ** -0.5, -BIG, ALU.mult, ALU.add)
                V.scalar_tensor_tensor(out=z[:, T + P:2 * T], in0=AUX[:, h % 2, T + P:2 * T], scalar=HD ** -0.5,
                                       in1=strict, op0=ALU.mult, op1=ALU.add).then_inc(sem("z3"), 1)

            masked_scores(0)
            for h in range(NH2):
                softplus(h)
                if h + 1 < NH2:
                    masked_scores(h + 1)
                log_weight(h)
                if h >= 2:
                    gated(h - 2, g0, "b")
            gated(NH2 - 2, g0, "b")
            gated(NH2 - 1, g0, "b")
            pending[0] = out_split("b", "o_b")
            phase("o_b", 4, evac=add_alpha("o_b"), then=layer_norm(1))
            embed(1, lambda: None)
            flush()
            dve.wait_ge(sem("x2_full"), 4)
            V.engine_nop().then_inc(sem("result"), 1)

        @block.tensor
        def _(pe):
            TE = nc.tensor

            def mm(out, lhs, rhs, start, stop):
                return TE.matmul(out, lhs, rhs, start=start, stop=stop, skip_group_check=True)

            def three(out, w_hi, w_lo, x_hi, x_lo, start, stop, weights_move=False):
                if weights_move:
                    mm(out, x_hi, w_hi, start, False)
                    mm(out, x_hi, w_lo, False, False)
                    return mm(out, x_lo, w_hi, False, stop)
                mm(out, w_hi, x_hi, start, False)
                mm(out, w_hi, x_lo, False, False)
                return mm(out, w_lo, x_hi, False, stop)

            def chunk_ready(c, reg=None, step=0):
                pe.wait_ge(lo_done, c + 1 if reg is None else reg * step + (c + 1))

            def acc_ready(g, reg=None, step=0):
                if g >= 2:
                    pe.wait_ge(acc_free, g - 1 if reg is None else reg * step + (g - 1))

            def group(c, g, xh, xl, reg=None, tiles=4, ks=(4, 4, 4, 4), width=512, weights_move=False,
                      extra=None, ready=None, up_groups=None):
                acc_ready(g, reg, 2)
                acc = ACC[g % 2]
                k0, K = 0, sum(ks)
                for j, nk in enumerate(ks):
                    cc = c + j
                    chunk_ready(cc, reg, 8)
                    for name in ready or ():
                        pe.wait_ge(sem(name), j + 1)
                    if up_groups:
                        pe.wait_ge(sem("up_done"), min(up_groups[0] + 2 * (j + 1), up_groups[1]))
                    hi = HI[cc % 2][:, 0:nk * width].rearrange("p (k n) -> p k n", n=width)
                    lo = LO[cc % 2][:, 0:nk * width].rearrange("p (k n) -> p k n", n=width)
                    for k in range(nk):
                        kk = k0 + k
                        first, last = kk == 0, kk == K - 1
                        if weights_move:
                            for t in range(2):
                                s = slice(P * t, P * t + P)
                                ins = three(acc[:, 2 * t:2 * t + 2, :].rearrange("p a b -> p (a b)"),
                                            hi[:, k, :], lo[:, k, :], xh[:, kk, s], xl[:, kk, s],
                                            first, last, weights_move=True)
                            continue
                        for t in range(tiles):
                            s = slice(P * t, P * t + P)
                            ins = three(acc[:, t, :], hi[:, k, s], lo[:, k, s], xh[:, kk, :], xl[:, kk, :],
                                        first and t % 2 == 0, last)
                        if extra:
                            ins = extra(hi, lo, k, kk, first, last)
                    ins.then_inc(pe_chunk, 1)
                    k0 += nk
                pe.wait_ge(pe_chunk, c + len(ks) if reg is None else reg * 8 + (c + len(ks)))
                pe.sem_inc(acc_full, 1)

            def ada_reduce(buf, fmas, outs):
                pe.wait_ge(ada_fma, fmas)
                pe.wait_ge(ada_out, outs)
                for t in range(4):
                    for i in range(2):
                        ins = mm(AUX[:, 3, t:t + 1], buf[:, i, P * t:P * t + P], ONES[:, 0:1], i == 0, i == 1)
                ins.then_inc(ada_sum, 1)

            def carry(name, g, reg=None):
                if name not in CARRY:
                    return
                first, per = CARRY[name]
                if per == 2:
                    if g == 0:
                        return
                    ag = first + (0 if reg is None else reg)
                    buf = FMA[0]
                else:
                    ag = first + g + (0 if reg is None else 2 * reg)
                    buf = FMA[(first + g) % 2]
                ada_reduce(buf, (ag - GTL) * 16 + 16, ag + TAKEN)

            def phase(name, n, ready=None, xh=AH, xl=AL, up_groups=None, **kw):
                c0, g0 = PH[name]
                if n == 1:
                    group(c0, g0, xh, xl, ready=ready, **kw)
                    carry(name, 0)
                    return
                with pe.Fori(0, n // 2) as i:
                    for g in range(2):
                        group(c0 + 4 * g, g0 + g, xh, xl, reg=i, ready=None if g else ready,
                              up_groups=None if g else up_groups, **kw)
                        carry(name, g, i)
                if n % 2:
                    group(c0 + 4 * (n - 1), g0 + n - 1, xh, xl, **kw)

            def totals(name, w, bank=0, ready="_ss", done="_tot"):
                pe.wait_ge(*since(name + ready, 1))
                mm(AUX[:, bank, 0:w], ONES[:, :], RSTD[:, 0:w], True, True).then_inc(step(name + done)[0], 1)

            pe.wait_ge(sem("ones"), 1)
            pe.wait_ge(sem("silu_c"), 1)
            both = SC[:, :].rearrange("p (v k) -> p k v", v=2)

            def ada_rows(par, reg=None, i=0):
                i = i if reg is None else reg
                if reg is not None or i:
                    pe.wait_ge(ada_row_out, i * 2 + (par - 1))
                for j in range(4):
                    pe.wait_ge(ada_full[j], i * 32 + 16 * (par + 1))
                    for k in range(4):
                        ins = mm(AUX[0:2, 1 + par, :], both[:, 4 * j + k, :], ADA[j][:, 512 * k:512 * k + 512],
                                 j == 0 and k == 0, j == 3 and k == 3)
                    ins.then_inc(ada_used, 1)
                pe.wait_ge(ada_used, i * 8 + 4 * (par + 1))
                pe.sem_inc(ada_row, 1)

            def ada_columns(par, reg=None, i=0):
                i = i if reg is None else reg
                pe.wait_ge(ada_row_out, i * 2 + (par + 1))
                for t in range(4):
                    ins = mm(AUX[:, 3, bass.ds(i * 16 + (8 * par + 2 * t), 2)], FMA[par][0:2, 0, P * t:P * t + P],
                             IDENT[0:2, 0:2], True, True)
                ins.then_inc(ada_sum, 1)

            ada_rows(0)
            ada_rows(1)
            totals("nx", T)
            pe.wait_ge(sem("consts_loaded"), 16)
            ada_columns(0)
            ada_rows(0, i=1)
            pe.wait_ge(*since("nx_std", 1))
            totals("nc", T)
            ada_columns(1)
            ada_rows(1, i=1)
            ada_columns(0, i=1)
            with pe.Fori(2, GTL // 2) as i:
                ada_rows(0, i)
                ada_columns(1, i - 1)
                ada_rows(1, i)
                ada_columns(0, i)
            ada_columns(1, i=GTL // 2 - 1)


            def context(hi, lo, k, kk, first, last):
                for t in range(3):
                    s = slice(P * t, P * t + P)
                    o = AUX[:, t // 2, T * (t % 2):T * (t % 2) + T]
                    ins = three(o, hi[:, k, s], lo[:, k, s], UH[:, kk, :], UL[:, kk, :], first and t % 2 == 0, last)
                return ins
            phase("kv_in", 1, tiles=3, width=384, extra=context, ready=("in_ready", "ctx_ready"))
            phase("q_in", 1)
            totals("nkv", 512)
            pe.wait_ge(*since("nkv_std", 1))
            totals("nq", T)
            pe.wait_ge(sem("consts_loaded"), 16)
            pe.wait_ge(sem("kr_copied"), 1)
            mm(AUX[:, 1, 0:T], con("rot1"), KR[:, 0:T], True, True).then_inc(sem("kr_rot"), 1)
            phase("conv_in", 6)
            c0, g0 = PH["q_b"]
            pe.wait_ge(sem("q_ready"), 1)
            for i in range(4):
                group(c0 + i, g0 + i, QH, QL, tiles=3, ks=(4,), width=384)
            c0, g0 = PH["kv_b"]
            pe.wait_ge(sem("kv_ready"), 1)
            for half in range(2):
                c = c0 + half
                chunk_ready(c)
                hi = HI[c % 2][:, :].rearrange("p (k n) -> p k n", k=2)
                lo = LO[c % 2][:, :].rearrange("p (k n) -> p k n", k=2)
                for i in range(4):
                    g = g0 + 4 * half + i
                    acc_ready(g)
                    a = ACC[g % 2][:, :, :].rearrange("p a b -> p (a b)")
                    for k in range(2):
                        for t in range(2):
                            o = a[:, 512 * t:512 * t + 512]
                            if half == 0:
                                s = slice(P * (2 * i + t), P * (2 * i + t) + P)
                                ins = three(o, hi[:, k, s], lo[:, k, s], KVH[:, k, :], KVL[:, k, :], k == 0, k == 1)
                            else:
                                s = slice(512 * t, 512 * t + 512)
                                q = slice(P * i, P * i + P)
                                ins = three(o, hi[:, k, s], lo[:, k, s], KVH[:, k, q], KVL[:, k, q], k == 0, k == 1,
                                            weights_move=True)
                    if i < 3:
                        ins.then_inc(acc_full, 1)
                    else:
                        ins.then_inc(pe_chunk, 1)
                        pe.wait_ge(pe_chunk, c + 1)
                        pe.sem_inc(acc_full, 1)
            pe.wait_ge(sem("qt1"), 1)
            for i in range(4):
                ins = mm(AUX[:, i // 2, T * (i % 2):T * (i % 2) + T], con("rot1"), QT1[:, 8 + i, :],
                         i % 2 == 0, i % 2 == 1)
            ins.then_inc(sem("q_rot"), 1)

            pe.wait_ge(sem("att1_in"), 1)
            g0 = PH["att1"][1]

            def scores(u):
                h, qt = u // 2, u % 2
                q = slice(P * qt, P * qt + P)
                r = slice(ROPE * (h % 2), ROPE * (h % 2) + ROPE)
                if u >= 2:
                    pe.wait_ge(sem("exp1"), u - 1)
                mm(AUX[:, u % 2, :], QT1[:, h, q], KN1[:, h, :], True, False)
                mm(AUX[:, u % 2, :], QT1[r, 8 + h // 2, q], KR[r, :], False, True).then_inc(sem("scores1"), 1)

            def turn(u):
                pe.wait_ge(sem("normed1"), u + 1)
                if u >= 2:
                    pe.wait_ge(sem("probs1"), u - 1)
                for k in range(4):
                    ins = TE.transpose(AUX[:, 2 + u % 2, P * k:P * k + P], PB[u % 4][:, P * k:P * k + P], IDENT)
                ins.then_inc(sem("turned1"), 1)

            def values(h):
                acc_ready(g0 + h)
                pe.wait_ge(sem("probs1"), 2 * h + 2)
                for k in range(4):
                    ins = mm(ACC[(g0 + h) % 2][:, 0, :], V1[:, k, P * h:P * h + P], PT[h % 2][:, k, :],
                             k == 0, k == 3)
                ins.then_inc(acc_full, 1)

            scores(0)
            scores(1)
            for u in range(2 * NH1):
                turn(u)
                if u + 2 < 2 * NH1:
                    scores(u + 2)
                if u % 2 == 0 and u:
                    values(u // 2 - 1)
            values(NH1 - 1)
            for b in range(4):
                pe.wait_ge(sem("mix_sq"), b + 1)
                if b >= 2:
                    pe.wait_ge(sem("mix_var"), b - 1)
                for i in range(2):
                    ins = mm(AUX[:, 2 * (b % 2) + i, :], ONES[:, :],
                             U[:, 16 + 4 * b + 2 * i:18 + 4 * b + 2 * i, :].rearrange("p a b -> p (a b)"), True, True)
                ins.then_inc(sem("mix_tot"), 1)
            pe.wait_ge(sem("mix_var"), 4)
            phase("w_out", 4, ready=("mix_ready",))
            totals("nf", T)
            for n, (a, b) in enumerate(PARTS):
                phase(f"up{n}", (b - a) // 2, ready=None if n else ("ffn_ready",))
                if (b - a) % 2:
                    full = (b - a) // 2
                    c0, g0 = PH[f"up{n}"]
                    group(c0 + 4 * full, g0 + full, AH, AL, tiles=2, ks=(8, 8), width=256)
                ups = (a // 2, (b + 1) // 2)
                if n < 2:
                    phase(f"down{n}", 4, xh=UH, xl=UL, up_groups=ups)
                else:
                    c0, g0 = PH[f"down{n}"]
                    for g in range(4):
                        group(c0 + 3 * g, g0 + g, UH, UL, ks=(4, 4, 3), up_groups=ups)
            totals("n2", T)
            pe.wait_ge(sem("consts2_loaded"), 16)
            pe.wait_ge(sem("minus_ones"), 1)
            c0, g0 = PH["ikw"]
            acc_ready(g0)
            for j in range(2):
                c = c0 + j
                chunk_ready(c)
                pe.wait_ge(sem("a_ready"), 2 * j + 2)
                hi = HI[c % 2][:, 0:8 * 144].rearrange("p (k n) -> p k n", n=144)
                lo = LO[c % 2][:, 0:8 * 144].rearrange("p (k n) -> p k n", n=144)
                for k in range(8):
                    kk = 8 * j + k
                    three(ACC[g0 % 2][:, 0, :], hi[:, k, 0:P], lo[:, k, 0:P], AH[:, kk, :], AL[:, kk, :],
                          kk == 0, kk == KD - 1)
                    for t in range(2):
                        s = slice(P * t, P * t + P)
                        ins = three(ACC[g0 % 2][:, 2, IH * t:IH * t + IH], hi[:, k, P:P + IH], lo[:, k, P:P + IH],
                                    AH[:, kk, s], AL[:, kk, s], kk == 0 and t == 0, kk == KD - 1, weights_move=True)
                ins.then_inc(pe_chunk, 1)
            pe.wait_ge(pe_chunk, c0 + 2)
            pe.sem_inc(acc_full, 1)
            phase("iq", 2)
            pe.wait_ge(sem("iq"), 1)
            pe.wait_ge(sem("ik"), 1)
            for b in range(3):
                if b == 2:
                    pe.wait_ge(sem("index_in"), 1)
                for t in range(4 if b < 2 else 1):
                    a = 2 * (b % 2) + t // 2
                    ins = mm(AUX[:, a, T * (t % 2):T * (t % 2) + T], con("roti"), Y[:, 4 + 4 * b + t, :],
                             t % 2 == 0, True)
                ins.then_inc(sem("index_rot"), 1)
            pe.wait_ge(sem("index_in"), 3)
            for u in range(IH):
                qt, pair = u // 8, u % 8
                if u >= 2:
                    pe.wait_ge(sem("index_relu"), u - 1)
                for i in range(2):
                    r = slice(ID * i, ID * i + ID)
                    ins = mm(AUX[:, 2 * (u % 2) + i, 0:T], Y[r, 4 + pair, P * qt:P * qt + P], Y[r, 12, :],
                             True, True)
                ins.then_inc(sem("index_dots"), 1)
            phase("k_a", 1)
            phase("v_a", 1, weights_move=True)
            phase("q_a", 4)
            phase("gate_a", 4)
            pe.wait_ge(sem("gate_a"), 1)
            pe.wait_ge(sem("index_relu"), IH)
            for b in range(5):
                if b >= 2:
                    pe.wait_ge(sem("a_in"), b - 1)
                for t in range(4):
                    x = Y[:, t, :] if b == 0 else U[:, 4 * b - 4 + t, :]
                    ins = mm(AUX[:, 2 * (b % 2) + t // 2, T * (t % 2):T * (t % 2) + T], con("rot2"), x,
                             t % 2 == 0, True)
                ins.then_inc(sem("a_rot"), 1)
            pe.wait_ge(sem("a_in"), 5)
            g0 = PH["att2"][1]

            def scores2(h):
                if h >= 2:
                    pe.wait_ge(sem("max2"), h - 1)
                for qt in range(2):
                    ins = mm(AUX[:, h % 2, T * qt:T * qt + T], U[:, h, P * qt:P * qt + P], Y[:, h // 4, :],
                             qt == 0, True)
                ins.then_inc(sem("scores2"), 1)

            def turn2(h):
                pe.wait_ge(sem("normed2"), h + 1)
                if h >= 2:
                    pe.wait_ge(sem("probs2"), h - 1)
                for kt in range(2):
                    for qt in range(2):
                        ins = TE.transpose(AUX[:, 2 + h % 2, T * kt + P * qt:T * kt + P * qt + P],
                                           PB[h % 4][:, T * qt + P * kt:T * qt + P * kt + P], IDENT)
                ins.then_inc(sem("turned2"), 1)

            def values2(h, w, ready, count):
                acc_ready(g0 + h)
                pe.wait_ge(*since(ready, count))
                for kt in range(2):
                    ins = mm(ACC[(g0 + h) % 2][:, 0, :], R0[:, 512 * kt + P * (h // 4):512 * kt + P * (h // 4) + P],
                             w(kt), kt == 0, kt == 1)
                ins.then_inc(acc_full, 1)

            scores2(0)
            scores2(1)
            for h in range(NH2):
                turn2(h)
                if h + 2 < NH2:
                    scores2(h + 2)
                if h:
                    values2(h - 1, lambda kt: PT2[(h - 1) % 2][:, kt, :], "probs2", h)
            values2(NH2 - 1, lambda kt: PT2[(NH2 - 1) % 2][:, kt, :], "probs2", NH2)
            phase("o_a", 4, ready=("att_ready_a",))

            def norm_sums(i):
                totals(f"ln{i}", T, bank=1, ready="_sum", done="_mean")
                totals(f"ln{i}", T)

            def embed(i):
                norm_sums(i)
                phase(f"pgate{i}", 4, ready=(f"ln{i}_ready",))
                c0, g0 = PH[f"ple{i}"]
                if i == 0:
                    pe.wait_ge(sem("p_ready"), 1)
                for j in range(2):
                    c = c0 + j
                    chunk_ready(c)
                    hi = HI[c % 2][:, :].rearrange("p (k n) -> p k n", k=2)
                    lo = LO[c % 2][:, :].rearrange("p (k n) -> p k n", k=2)
                    for half in range(2):
                        g = g0 + 2 * j + half
                        acc_ready(g)
                        for k in range(2):
                            for t in range(4):
                                s = slice(512 * half + P * t, 512 * half + P * t + P)
                                ins = three(ACC[g % 2][:, t, :], hi[:, k, s], lo[:, k, s], PTH[:, 2 * i + k, :],
                                            PTL[:, 2 * i + k, :], k == 0 and t % 2 == 0, k == 1)
                        if half == 0:
                            ins.then_inc(acc_full, 1)
                        else:
                            ins.then_inc(pe_chunk, 1)
                            pe.wait_ge(pe_chunk, c + 1)
                            pe.sem_inc(acc_full, 1)
            embed(0)
            phase("k_b", 1, ready=("b_ready",))
            phase("v_b", 1, weights_move=True)
            phase("q_bb", 4)
            phase("gate_b", 4)
            pe.wait_ge(sem("gate_b"), 1)
            g0 = PH["att3"][1]

            def scores3(h):
                if h >= 2:
                    pe.wait_ge(sem("z3"), h - 1)
                for st in range(2):
                    ins = mm(AUX[:, h % 2, T * st:T * st + T], Y[:, h // 4, P * st:P * st + P], U[:, h, :],
                             st == 0, True)
                ins.then_inc(sem("scores3"), 1)

            def suffix3(h):
                pe.wait_ge(sem("sp3"), h + 1)
                a, sp = AUX[:, 2 + h % 2, :], PB[h % 4]
                mm(a[:, 0:T], con("tri"), sp[:, 0:T], True, False)
                mm(a[:, 0:T], MINUS[:, :], sp[:, T:2 * T], False, True)
                mm(a[:, T:2 * T], con("tri"), sp[:, T:2 * T], False, True).then_inc(sem("suffix3"), 1)

            scores3(0)
            scores3(1)
            for h in range(NH2):
                suffix3(h)
                if h + 2 < NH2:
                    scores3(h + 2)
                if h:
                    values2(h - 1, lambda kt: PB[(h - 1) % 4][:, T * kt:T * kt + T], "exp3", h)
            values2(NH2 - 1, lambda kt: PB[(NH2 - 1) % 4][:, T * kt:T * kt + T], "exp3", NH2)
            phase("o_b", 4, ready=("att_ready_b",))
            embed(1)


def _constants():
    out = np.zeros((P, NCON), np.float32)

    def put(name, a):
        at, n = CON[name]
        out[:, at:at + n] = a

    put("ident", np.eye(P))
    rot1 = np.zeros((P, P))
    for i in range(0, P, 2):
        rot1[i + 1, i] = -1.0
        rot1[i, i + 1] = 1.0
    put("rot1", rot1)
    rot2 = np.zeros((P, P))
    half = HD // 8
    for i in range(half):
        rot2[half + i, i] = -1.0
        rot2[i, half + i] = 1.0
    put("rot2", rot2)
    roti = np.zeros((P, P))
    ih = ID // 8
    for b in (0, ID):
        for i in range(ih):
            roti[b + ih + i, b + i] = -1.0
            roti[b + i, b + ih + i] = 1.0
    put("roti", roti)
    f = np.float32
    axis = ROPE // 2
    inv = f(10000.0) ** (-np.arange(0, axis, 2, dtype=f) / f(axis))
    t = np.arange(T)
    ang = np.concatenate([(t // 64).astype(f)[:, None] * inv, (t % 64).astype(f)[:, None] * inv], axis=-1)
    ang = ang.astype(f).astype(np.float64)
    lane = (np.arange(P) % ROPE) // 2
    put("cos1", np.cos(ang).T[lane])
    put("sin1", np.sin(ang).T[lane])
    put("tri", -(np.arange(P)[:, None] >= np.arange(P)[None, :]).astype(f))
    put("strict", np.where(np.arange(P)[:, None] < np.arange(P)[None, :], 0.0, -BIG))

    def freq(n):
        return (f(1.0) / (f(THETA) ** (np.arange(n, dtype=f) / f(n)))).astype(f)
    a = np.zeros((P, 1), f)
    a[0:half, 0] = a[half:2 * half, 0] = freq(half)
    put("inv2", a)
    a = np.zeros((P, 1), f)
    for b in (0, ID):
        a[b:b + ih, 0] = a[b + ih:b + 2 * ih, 0] = freq(ih)
    put("invi", a)
    put("half_pi", np.pi / 2)
    return out


def kernel(**inputs):
    import concourse.bacc as bacc
    from concourse import mybir
    from concourse.bass_utils import run_bass_kernel_spmd

    arr = {k: np.asarray(v) for k, v in inputs.items()}
    F32 = np.float32

    chunks, _ = schedule()
    stream = np.zeros((len(chunks), P, CHUNK), F32)
    for c, spec in enumerate(chunks):
        if spec is None:
            continue
        key, layer, ks, cols = spec
        w = arr[key]
        w = w[layer] if w.ndim == 3 else w
        rows = w[ks[0] * P:(ks[-1] + 1) * P].reshape(len(ks), P, -1)
        part = np.concatenate([rows[:, :, a:b] for a, b in cols], axis=2).transpose(1, 0, 2).reshape(P, -1)
        stream[c, :, :part.shape[1]] = part
    ada = arr["w_ada"][0].reshape(4, 4, P, 24, 512).transpose(3, 0, 2, 1, 4).reshape(96, P, CHUNK)

    def col(a):
        return a.reshape(-1, P).T

    vecs = np.zeros((P, NVEC), F32)

    def put(name, a):
        at, n = VEC[name]
        vecs[:, at:at + n] = a

    put("c", col(arr["c"][0]))
    put("c_ctx", col(arr["c_ctx"]))
    put("b_ada", col(arr["b_ada"][0]))
    for name in ("g_mix_norm", "g_q_a", "g_kv_a", "g_mix_out", "g_ffn_norm"):
        put(name, col(arr[name][0]))
    put("g_final", col(arr["g_final"]))
    put("ln_g", col(arr["ln_g_2"].reshape(-1)))
    put("ln_b", col(arr["ln_b_2"].reshape(-1)))
    taps = np.stack([col(arr["conv_w"][0, i]) for i in range(3)] + [col(arr["conv_b"][0])], axis=2)
    put("conv", taps.reshape(P, -1))
    taps = np.stack([col(arr["ffn_conv_w"][0, i]) for i in range(3)] + [col(arr["ffn_conv_b"][0])], axis=2)
    a, g = taps[:, :FT], taps[:, FT:]
    order = []
    for f in range(0, FT, 2):
        n = min(2, FT - f)
        if n == 2:
            order += [a[:, f], a[:, f + 1], g[:, f], g[:, f + 1]]
        else:
            order += [a[:, f], np.zeros((P, 4), F32), g[:, f], np.zeros((P, 4), F32)]
    order = np.concatenate(order, axis=1)
    put("ffn_conv", np.pad(order, ((0, 0), (0, 0)))[:, :VEC["ffn_conv"][1]])

    def tokens(a):
        return np.ascontiguousarray(a.reshape(T, -1, P).transpose(2, 1, 0))

    p = arr["p_2"]
    data = {
        "stream": stream,
        "ada_stream": np.ascontiguousarray(ada),
        "vecs": vecs,
        "consts": _constants(),
        "x_t": tokens(arr["x"][0]),
        "ctx_t": tokens(arr["ctx"][0]),
        "p_t": np.concatenate([tokens(p[0, 0]), tokens(p[1, 0])], axis=1).reshape(P, 4 * T),
        "positions": np.broadcast_to(arr["positions_2"].reshape(1, T), (P, T)).copy(),
    }
    nc = bacc.Bacc("TRN2", target_bir_lowering=False, num_devices=1)
    args = [nc.dram_tensor(n, a.shape, mybir.dt.from_np(a.dtype), kind="ExternalInput").ap()
            for n, a in data.items()]
    out = nc.dram_tensor("out", (P, KD, T), mybir.dt.float32, kind="ExternalOutput").ap()
    two_blocks(nc, *args, out)
    r = run_bass_kernel_spmd(nc, [data], core_ids=[0])
    return r.results[0]["out"].transpose(2, 1, 0).reshape(1, T, D)
```
